# Optimizing a Trainium2 kernel written in Bass

```python
import jax, jax.numpy as jnp
from jax import lax
import numpy as np

D_MODEL = 1024
BATCH = 1
SEQ = 1024
DEPTH = 1
DEC_BATCH = 8
DEC_SEQ = 1
PAST_LEN = 4096
PAGE_SIZE = 128

MLA_HEADS = 8
Q_LORA = 384
KV_LORA = 256
QK_NOPE = 64
QK_ROPE = 32
V_HEAD = 64
Q_BLOCK = 128
RET_HEADS = 4
RET_DK = 128
RET_DV = 256
RET_CHUNK = 128
PEER_HEADS = 8
N_KEYS = 128
N_EXPERTS = N_KEYS * N_KEYS
PEER_DQ = 256
PEER_TOPK = 16
PEER_BLOCK = 128

ROPE_BASE = 10000.0
EPS = 1e-6
IN_WIDTH = Q_LORA + KV_LORA + QK_ROPE + 2 * RET_HEADS * RET_DK + 2 * RET_HEADS * RET_DV + 2 * D_MODEL

kernel_name = 'hybrid_mla_retention_peer_step'

def rms_norm(x, g):
    xf = x.astype(jnp.float32)
    y = xf * lax.rsqrt(jnp.mean(xf * xf, axis=-1, keepdims=True) + EPS)
    return (y * g.astype(jnp.float32)).astype(x.dtype)

def rope(x, pos):
    d = x.shape[-1]
    inv = ROPE_BASE ** (-jnp.arange(0, d, 2, dtype=jnp.float32) / d)
    ang = pos.astype(jnp.float32)[:, None] * inv[None, :]
    cos = jnp.cos(ang)[None, :, None, :]
    sin = jnp.sin(ang)[None, :, None, :]
    x1 = x[..., : d // 2].astype(jnp.float32)
    x2 = x[..., d // 2:].astype(jnp.float32)
    return jnp.concatenate([x1 * cos - x2 * sin, x1 * sin + x2 * cos], axis=-1).astype(x.dtype)

def split_combined(z):
    sizes = (Q_LORA, KV_LORA, QK_ROPE, RET_HEADS * RET_DK, RET_HEADS * RET_DK,
             RET_HEADS * RET_DV, RET_HEADS * RET_DV, D_MODEL, D_MODEL)
    out, off = [], 0
    for s in sizes:
        out.append(z[..., off:off + s])
        off += s
    return out

def retention_log_gamma():
    return jnp.log1p(-jnp.exp2(-5.0 - jnp.arange(RET_HEADS, dtype=jnp.float32)))

def mixer_projections(xn, pos, w_in, q_norm_g, w_uq, kv_norm_g, w_uk):
    B, S, _ = xn.shape
    q_lat, ckv, krope, rq, rk, rv, rg, ga, gb = split_combined(xn @ w_in)
    q = (rms_norm(q_lat, q_norm_g) @ w_uq).reshape(B, S, MLA_HEADS, QK_NOPE + QK_ROPE)
    q_abs = jnp.einsum('bshn,chn->bshc', q[..., :QK_NOPE], w_uk)
    q_pe = rope(q[..., QK_NOPE:], pos)
    ckv = rms_norm(ckv, kv_norm_g)
    krope = rope(krope[:, :, None, :], pos)[:, :, 0]
    rq = rope(rq.reshape(B, S, RET_HEADS, RET_DK), pos).transpose(0, 2, 1, 3)
    rk = (rope(rk.reshape(B, S, RET_HEADS, RET_DK), pos) * (RET_DK ** -0.5)).transpose(0, 2, 1, 3)
    rv = rv.reshape(B, S, RET_HEADS, RET_DV).transpose(0, 2, 1, 3)
    return q_abs, q_pe, ckv, krope, rq, rk, rv, rg, ga, gb

def mla_attend(q_abs, q_pe, ckv, krope, mask):
    scale = (QK_NOPE + QK_ROPE) ** -0.5
    s = (jnp.einsum('bqhc,bkc->bhqk', q_abs, ckv)
         + jnp.einsum('bqhr,bkr->bhqk', q_pe, krope)).astype(jnp.float32) * scale
    s = jnp.where(mask[None, None], s, -jnp.inf)
    p = jax.nn.softmax(s, axis=-1).astype(ckv.dtype)
    return jnp.einsum('bhqk,bkc->bqhc', p, ckv)

def mla_prompt(q_abs, q_pe, ckv, krope):
    B, S = q_abs.shape[:2]
    kpos = jnp.arange(S)

    def block(i):
        start = i * Q_BLOCK
        qa = lax.dynamic_slice_in_dim(q_abs, start, Q_BLOCK, axis=1)
        qp = lax.dynamic_slice_in_dim(q_pe, start, Q_BLOCK, axis=1)
        qpos = start + jnp.arange(Q_BLOCK)
        return mla_attend(qa, qp, ckv, krope, kpos[None, :] <= qpos[:, None])

    o = lax.map(block, jnp.arange(S // Q_BLOCK))
    return o.transpose(1, 0, 2, 3, 4).reshape(B, S, MLA_HEADS, KV_LORA)

def retention_chunk(state, q, k, v, log_gamma):
    L = q.shape[2]
    i = jnp.arange(L, dtype=jnp.float32)
    lg = log_gamma[:, None, None]
    rel = i[:, None] - i[None, :]
    decay = jnp.where(rel >= 0, jnp.exp(jnp.maximum(rel, 0.0) * lg), 0.0).astype(q.dtype)
    o = jnp.einsum('bhij,bhje->bhie', jnp.einsum('bhid,bhjd->bhij', q, k) * decay, v)
    q_decay = jnp.exp((i + 1.0)[None, :, None] * lg).astype(q.dtype)
    o = o + jnp.einsum('bhid,bhde->bhie', q, state) * q_decay
    k_decay = jnp.exp((L - 1.0 - i)[None, :, None] * lg).astype(q.dtype)
    chunk_decay = jnp.exp(L * log_gamma)[:, None, None].astype(q.dtype)
    new_state = chunk_decay * state + jnp.einsum('bhjd,bhje->bhde', k * k_decay, v)
    return new_state.astype(state.dtype), o

def retention_prompt(q, k, v, log_gamma):
    B, H, S, _ = q.shape
    nc = S // RET_CHUNK

    def to_chunks(a):
        return a.reshape(B, H, nc, RET_CHUNK, a.shape[-1]).transpose(2, 0, 1, 3, 4)

    state0 = jnp.zeros((B, H, RET_DK, RET_DV), q.dtype)

    def step(st, qkv):
        return retention_chunk(st, qkv[0], qkv[1], qkv[2], log_gamma)

    st, o = lax.scan(step, state0, (to_chunks(q), to_chunks(k), to_chunks(v)))
    return o.transpose(1, 2, 0, 3, 4).reshape(B, H, S, RET_DV), st

def head_group_norm(o, g):
    B, S = o.shape[:2]
    of = o.astype(jnp.float32)
    mu = jnp.mean(of, axis=-1, keepdims=True)
    c = of - mu
    y = c * lax.rsqrt(jnp.mean(c * c, axis=-1, keepdims=True) + EPS)
    return (y.reshape(B, S, RET_HEADS * RET_DV) * g.astype(jnp.float32)).astype(o.dtype)

def merge_branches(o_lat, o_ret, rg, ga, gb, w_uv, ret_norm_g, w_oa, w_ob, w_out):
    B, S = o_lat.shape[:2]
    o_a = jnp.einsum('bshc,chv->bshv', o_lat, w_uv).reshape(B, S, MLA_HEADS * V_HEAD) @ w_oa
    o_b = (jax.nn.silu(rg) * head_group_norm(o_ret.transpose(0, 2, 1, 3), ret_norm_g)) @ w_ob
    return (jax.nn.sigmoid(ga) * o_a + jax.nn.sigmoid(gb) * o_b) @ w_out

def peer(xn, w_q, sub_keys, expert_u, expert_v):
    B, S, D = xn.shape
    T = B * S
    nblk = -(-T // PEER_BLOCK)
    t = jnp.pad(xn.reshape(T, D), ((0, nblk * PEER_BLOCK - T), (0, 0))).reshape(nblk, PEER_BLOCK, D)

    def block(tb):
        q = (tb @ w_q).reshape(PEER_BLOCK, PEER_HEADS, 2, PEER_DQ // 2).astype(jnp.float32)
        q = q * lax.rsqrt(jnp.mean(q * q, axis=-1, keepdims=True) + EPS)
        s = jnp.einsum('thpd,phkd->thpk', q, sub_keys.astype(jnp.float32))
        sv, si = lax.top_k(s, PEER_TOPK)
        cand = (sv[:, :, 0, :, None] + sv[:, :, 1, None, :]).reshape(PEER_BLOCK, PEER_HEADS, PEER_TOPK * PEER_TOPK)
        cid = (si[:, :, 0, :, None] * N_KEYS + si[:, :, 1, None, :]).reshape(PEER_BLOCK, PEER_HEADS, PEER_TOPK * PEER_TOPK)
        top_s, top_pos = lax.top_k(cand, PEER_TOPK)
        eid = jnp.take_along_axis(cid, top_pos, axis=-1)
        g = jax.nn.softmax(top_s, axis=-1).astype(tb.dtype)
        act = jax.nn.gelu(jnp.einsum('thkd,td->thk', expert_u[eid], tb))
        return jnp.einsum('thk,thkd->td', g * act, expert_v[eid])

    return lax.map(block, t).reshape(nblk * PEER_BLOCK, D)[:T].reshape(B, S, D)

def setup_inputs(seed: int = 0) -> dict:
    key = jax.random.key(seed)
    ks = jax.random.split(key, 24)
    f32 = jnp.float32
    n_pages = PAST_LEN // PAGE_SIZE
    n_phys = (DEC_BATCH * n_pages * 5) // 4

    def nrm(k, shape, scale):
        return jax.random.normal(k, shape, f32) * scale

    def gain(k, shape):
        return 1.0 + 0.02 * jax.random.normal(k, shape, f32)

    page_table = jax.random.permutation(ks[5], n_phys)[: DEC_BATCH * n_pages].reshape(DEC_BATCH, n_pages).astype(jnp.int32)
    return {
        'x_prompt': nrm(ks[0], (BATCH, SEQ, D_MODEL), 1.0),
        'x_sample': nrm(ks[1], (DEC_BATCH, DEC_SEQ, D_MODEL), 1.0),
        'cache_ckv': nrm(ks[2], (DEPTH, n_phys, PAGE_SIZE, KV_LORA), 1.0),
        'cache_krope': nrm(ks[3], (DEPTH, n_phys, PAGE_SIZE, QK_ROPE), 1.0),
        'state_ret': nrm(ks[4], (DEPTH, DEC_BATCH, RET_HEADS, RET_DK, RET_DV), RET_DK ** -0.5),
        'page_table': page_table,
        'attn_norm_g': gain(ks[6], (DEPTH, D_MODEL)),
        'w_in': nrm(ks[7], (DEPTH, D_MODEL, IN_WIDTH), D_MODEL ** -0.5),
        'q_norm_g': gain(ks[8], (DEPTH, Q_LORA)),
        'w_uq': nrm(ks[9], (DEPTH, Q_LORA, MLA_HEADS * (QK_NOPE + QK_ROPE)), Q_LORA ** -0.5),
        'kv_norm_g': gain(ks[10], (DEPTH, KV_LORA)),
        'w_uk': nrm(ks[11], (DEPTH, KV_LORA, MLA_HEADS, QK_NOPE), KV_LORA ** -0.5),
        'w_uv': nrm(ks[12], (DEPTH, KV_LORA, MLA_HEADS, V_HEAD), KV_LORA ** -0.5),
        'ret_norm_g': gain(ks[13], (DEPTH, RET_HEADS * RET_DV)),
        'w_oa': nrm(ks[14], (DEPTH, MLA_HEADS * V_HEAD, D_MODEL), (MLA_HEADS * V_HEAD) ** -0.5),
        'w_ob': nrm(ks[15], (DEPTH, RET_HEADS * RET_DV, D_MODEL), (RET_HEADS * RET_DV) ** -0.5),
        'w_out': nrm(ks[16], (DEPTH, D_MODEL, D_MODEL), D_MODEL ** -0.5),
        'ffn_norm_g': gain(ks[17], (DEPTH, D_MODEL)),
        'peer_w_q': nrm(ks[18], (DEPTH, D_MODEL, PEER_HEADS * PEER_DQ), D_MODEL ** -0.5),
        'peer_sub_keys': nrm(ks[19], (DEPTH, 2, PEER_HEADS, N_KEYS, PEER_DQ // 2), (PEER_DQ // 2) ** -0.5),
        'peer_u': nrm(ks[20], (DEPTH, N_EXPERTS, D_MODEL), D_MODEL ** -0.5),
        'peer_v': nrm(ks[21], (DEPTH, N_EXPERTS, D_MODEL), PEER_HEADS ** -0.5),
        'final_norm_g': gain(ks[22], (D_MODEL,)),
    }

def reference(x_prompt, x_sample, cache_ckv, cache_krope, state_ret, page_table,
              attn_norm_g, w_in, q_norm_g, w_uq, kv_norm_g, w_uk, w_uv, ret_norm_g,
              w_oa, w_ob, w_out, ffn_norm_g, peer_w_q, peer_sub_keys, peer_u, peer_v,
              final_norm_g):
    log_gamma = retention_log_gamma()
    B, S, _ = x_prompt.shape
    DB, DS, _ = x_sample.shape
    past_len = page_table.shape[1] * cache_ckv.shape[2]
    pos_p = jnp.arange(S)
    pos_s = past_len + jnp.arange(DS)
    kpos_s = jnp.arange(past_len + DS)
    mask_s = kpos_s[None, :] <= pos_s[:, None]

    hp, hs = x_prompt, x_sample
    ckv_p_l, kr_p_l, st_p_l, ckv_s_l, kr_s_l, st_s_l = [], [], [], [], [], []
    for l in range(DEPTH):
        xn = rms_norm(hp, attn_norm_g[l])
        q_abs, q_pe, ckv, krope, rq, rk, rv, rg, ga, gb = mixer_projections(
            xn, pos_p, w_in[l], q_norm_g[l], w_uq[l], kv_norm_g[l], w_uk[l])
        o_lat = mla_prompt(q_abs, q_pe, ckv, krope)
        o_ret, st_p = retention_prompt(rq, rk, rv, log_gamma)
        hp = hp + merge_branches(o_lat, o_ret, rg, ga, gb, w_uv[l], ret_norm_g[l], w_oa[l], w_ob[l], w_out[l])
        hp = hp + peer(rms_norm(hp, ffn_norm_g[l]), peer_w_q[l], peer_sub_keys[l], peer_u[l], peer_v[l])
        ckv_p_l.append(ckv.reshape(B, S // PAGE_SIZE, PAGE_SIZE, KV_LORA))
        kr_p_l.append(krope.reshape(B, S // PAGE_SIZE, PAGE_SIZE, QK_ROPE))
        st_p_l.append(st_p)

        xn = rms_norm(hs, attn_norm_g[l])
        q_abs, q_pe, ckv, krope, rq, rk, rv, rg, ga, gb = mixer_projections(
            xn, pos_s, w_in[l], q_norm_g[l], w_uq[l], kv_norm_g[l], w_uk[l])
        ckv_all = jnp.concatenate([cache_ckv[l][page_table].reshape(DB, past_len, KV_LORA), ckv], axis=1)
        kr_all = jnp.concatenate([cache_krope[l][page_table].reshape(DB, past_len, QK_ROPE), krope], axis=1)
        o_lat = mla_attend(q_abs, q_pe, ckv_all, kr_all, mask_s)
        st_s, o_ret = retention_chunk(state_ret[l], rq, rk, rv, log_gamma)
        hs = hs + merge_branches(o_lat, o_ret, rg, ga, gb, w_uv[l], ret_norm_g[l], w_oa[l], w_ob[l], w_out[l])
        hs = hs + peer(rms_norm(hs, ffn_norm_g[l]), peer_w_q[l], peer_sub_keys[l], peer_u[l], peer_v[l])
        ckv_s_l.append(ckv)
        kr_s_l.append(krope)
        st_s_l.append(st_s)

    y_prompt = rms_norm(hp, final_norm_g)
    y_sample = rms_norm(hs, final_norm_g)
    return (y_prompt, y_sample,
            jnp.stack(ckv_p_l, 0), jnp.stack(kr_p_l, 0), jnp.stack(st_p_l, 0),
            jnp.stack(ckv_s_l, 0), jnp.stack(kr_s_l, 0), jnp.stack(st_s_l, 0))


_drawn_inputs = setup_inputs


def setup_inputs(seed=0):
    import zlib

    import numpy as np

    out = dict(_drawn_inputs(seed))
    spreads = {}
    factors = {'cache_krope': 2.79,
     'q_norm_g': 8.0,
     'kv_norm_g': 2.738,
     'ret_norm_g': 10.425,
     'final_norm_g': 7.679,
     'ffn_norm_g': 4.343}
    for name, (base, spread) in spreads.items():
        noise = np.random.default_rng([zlib.crc32(name.encode()), seed]).standard_normal(out[name].shape)
        drawn = base * np.exp(spread * noise) if base else spread * noise
        out[name] = __import__('jax').numpy.asarray(drawn.astype(out[name].dtype))
    for name, factor in factors.items():
        out[name] = (out[name] * factor).astype(out[name].dtype)
    return out
```

```python
from contextlib import ExitStack

import numpy as np
import concourse.bass as bass
from concourse import mybir

ALU = mybir.AluOpType
ACT = mybir.ActivationFunctionType
F32 = mybir.dt.float32
I32 = mybir.dt.int32
U32 = mybir.dt.uint32
AX = mybir.AxisListType.X
ds = bass.ds

P = 128
EPS = 1e-6
ROPE_BASE = 10000.0
TOPK = 16
NEG = -1e30
GELU_C = float(np.sqrt(2.0 / np.pi))
GELU_A = 0.044715
RSQRT_MAGIC = 1597463007.0


class Signal:

    def __init__(self, sem, per):
        self.sem, self.per = sem, per

    def wait(self, eng, t, k=None):
        value = t * self.per + (self.per if k is None else k)
        if isinstance(value, int) and value <= 0:
            return
        eng.wait_ge(self.sem, value)


class Link:

    def __init__(self, sem, name, per):
        self.sem, self.name, self.per, self.t, self.k, self.dirty = sem, name, per, 0, 0, False

    def begin(self, t):
        self.t, self.k = t, 0

    def __call__(self, eng, ins):
        ins.then_inc(self.sem, 1)
        self.k += 1
        eng.wait_ge(self.sem, self.t * self.per + self.k)

    def mark(self, ins):
        ins.then_inc(self.sem, 1)
        self.k += 1

    def join(self, eng):
        eng.wait_ge(self.sem, self.t * self.per + self.k)

    def end(self):
        assert self.k == self.per, (self.name, "links in a round:", self.k, "declared:", self.per)


class Jobs:

    def __init__(self, filled, drained, names, banks, blocks, rounds=1, before=None):
        self.filled, self.drained, self.banks, self.before, self.blocks = filled, drained, banks, before, blocks
        self.at, self.fills, self.per, self.fills_per = {}, {}, 0, 0
        for name, n in names:
            self.at[name], self.fills[name] = self.per, self.fills_per
            self.per += n
            self.fills_per += 0 if name in blocks else n
        self.total = rounds * self.per
        assert rounds == 1 or self.per % len(banks) == 0

    def bank(self, name, i=0):
        return self.banks[(self.at[name] + i) % len(self.banks)]

    def may_fill(self, pe, t, name, i=0):
        j = self.at[name] + i
        if self.before is not None and j < len(self.banks):
            pe.wait_ge(self.before.drained, self.before.total)
        value = t * self.per + j + 1 - len(self.banks)
        if not isinstance(value, int) or value > 0:
            pe.wait_ge(self.drained, value)

    def wait_filled(self, eng, t, name, i=0):
        assert name not in self.blocks
        eng.wait_ge(self.filled, t * self.fills_per + self.fills[name] + i + 1)

    def wait_drained(self, eng, t, name, i=0):
        value = t * self.per + self.at[name] + i + 1
        if not isinstance(value, int) or value > 0:
            eng.wait_ge(self.drained, value)


def program(nc, a, out, const):
    _, SEQ, D = a["x_prompt"].shape
    NB = a["x_sample"].shape[0]
    _, NPHYS, PAGE, KVL = a["cache_ckv"].shape
    ROPE = a["cache_krope"].shape[3]
    _, _, RH, RDK, RDV = a["state_ret"].shape
    NPAGES = a["page_table"].shape[1]
    QL = a["q_norm_g"].shape[1]
    NH = a["w_uk"].shape[2]
    NOPE = a["w_uk"].shape[3]
    VH = a["w_uv"].shape[3]
    _, _, PH, NK, PD = a["peer_sub_keys"].shape
    assert PAGE == P and NK == P and PD == P and RDK == P and D == 1024 and NB == 8
    HD = NOPE + ROPE
    T = SEQ // P
    KC = D // P
    QC = QL // P
    SCALE = float(HD) ** -0.5
    O_CKV, O_KR = QL, QL + KVL
    O_RQ = O_KR + ROPE
    O_RV = O_RQ + 2 * RH * RDK
    O_RG = O_RV + RH * RDV
    O_GA = O_RG + RH * RDV
    O_GB = O_GA + D
    HALVES = -(-SEQ // 512)
    HW = min(SEQ, 512)
    RING = 4

    w_in, w_uq, w_oa, w_ob, w_out, w_q = (a[n][0] for n in ("w_in", "w_uq", "w_oa", "w_ob", "w_out", "peer_w_q"))
    BW = 256
    stream = [("linA", w_in, c, min(BW, O_RG - c)) for c in range(0, O_RG, BW)]
    NA = len(stream)
    stream += [("uq", w_uq, c, BW) for c in range(0, NH * HD, BW)]
    stream += [("rg", w_in, O_RG + c, BW) for c in range(0, D, BW)]
    stream += [("ob", w_ob, c, BW) for c in range(0, D, BW)]
    stream += [("oa", w_oa, c, 512) for c in range(0, D, 512)]
    stream += [("gate", w_in, O_GA + c, BW) for c in range(0, 2 * D, BW)]
    stream += [("out", w_out, c, BW) for c in range(0, D, BW)]
    stream += [("wq", w_q, c, BW) for c in range(0, 2 * PH * PD, BW)]
    NBLK = len(stream)
    WSLOTS = 4
    assert NBLK % WSLOTS == 0
    first = {}
    for n, (name, _, _, _) in enumerate(stream):
        first.setdefault(name, n)

    with ExitStack() as ctx:
        def sb(name, words, dt=F32):
            return ctx.enter_context(nc.sbuf_tensor(name, [P, words], dt))

        def sem(name):
            return ctx.enter_context(nc.semaphore(name))

        def signal(name, per=1):
            return Signal(sem(name), per)

        def grid(ap, n):
            return ap.rearrange("p (a b) -> p a b", a=n)

        ident = sb("ident", P)
        ffn_gain = sb("ffn_gain", D)
        final_gain = sb("final_gain", D)
        kv_gain = sb("kv_gain", KVL)
        attn_gain_t = sb("attn_gain_t", KC)
        q_gain_t = sb("q_gain_t", QC)
        ret_gain_t = sb("ret_gain_t", KC)
        decay_t = sb("decay_t", RH * P)
        q_decay = sb("q_decay", RH * P)
        k_decay = sb("k_decay", RH)
        iota16 = sb("iota16", TOPK)
        diag8 = sb("diag8", NB * NB)
        ret_eye = sb("ret_eye", NB)
        uk = sb("uk", 2 * NH * NOPE)
        uv = sb("uv", 2 * NH * VH)
        keys_t = sb("keys_t", 2 * PH * P)
        pages_reg = sb("pages_reg", NB * NPAGES, I32)
        KV = sb("KV", max(NH * SEQ, NPAGES * KVL) + max(T * NH * VH, NPAGES * ROPE + 3072))
        VAT = max(NH * SEQ, NPAGES * KVL)
        key_t = KV[:, 0:NH * SEQ].rearrange("p (h s) -> p h s", h=NH)
        value = KV[:, VAT:VAT + T * NH * VH].rearrange("p (t c) -> p t c", t=T)
        state = sb("state", RH * RDV)
        rows = sb("rows", RING * D)
        wbuf = sb("wbuf", WSLOTS * KC * BW)
        px = sb("px", D)
        py = [sb("py0", D), sb("py1", D)]
        pe_id = sb("pe_id", P, U32)
        pe_id_s = [sb(f"pe_id_s{i}", TOPK, U32) for i in range(2)]
        pg = sb("pg", P)
        dots = sb("dots", TOPK)
        ga_, gb_, gcoef = sb("ga_", TOPK), sb("gb_", TOPK), sb("gcoef", TOPK)
        fin = sb("fin", 8)
        xin = sb("xin", D)
        xt = sb("xt", D)
        z = sb("z", O_RG)
        WK = sb("WK", max(4 * D, NPAGES * P) + 8)
        sc = [WK[:, 0:D], WK[:, 3 * D:4 * D]]
        pt = WK[:, D:2 * D]
        maskb = WK[:, 2 * D:3 * D]
        xn2 = maskb
        oa = WK[:, 3 * D:4 * D]
        rqk = WK[:, 3 * D:4 * D]
        rqt, rqd, rkt, kd = (WK[:, i * 512:(i + 1) * 512] for i in range(4))
        at = WK[:, 3 * D:3 * D + 512]
        t2 = sb("t2", D)
        oret = sb("oret", D)
        qb = sb("qb", NH * HD)
        knat = sb("knat", NH * HD)
        qt = sb("qt", NH * P)
        ropeb = sb("ropeb", 3 * (RDK // 2) + 3 * (ROPE // 2))
        rt = sb("rt", 2 * NH * ROPE)
        stat = sb("stat", 16)
        nr = sb("nr", 48)
        mx, nmx, sums = sb("mx", NH), sb("nmx", NH), sb("sums", NH)
        rstat = sb("rstat", 4 * RH)
        ssq = sb("ssq", 2 * PH)
        rstd_q = sb("rstd_q", 2 * PH)
        sv = sb("sv", 2 * PH * TOPK)
        si = sb("si", 2 * PH * TOPK, U32)
        sif = sb("sif", 2 * PH * TOPK)
        ts_ = sb("ts_", P)
        tp = sb("tp", P, U32)
        tq = sb("tq", P, U32)
        tf = sb("tf", P)
        i0, i1 = sb("i0", P), sb("i1", P)
        eid = sb("eid", P, U32)
        gw = sb("gw", P)
        gs = sb("gs", 2 * PH)
        qs = sb("qs", 3 * NH + 3)
        cuts = [0]

        def cut(words):
            cuts.append(cuts[-1] + words)
            assert cuts[-1] <= NH * P
            return qt[:, cuts[-2]:cuts[-1]]

        qabs = cut(3 * NH * NB)
        nkr = cut(NB)
        qmb = cut(RH * NB)
        ptb = cut(NPAGES * NH)
        psl = cut(2 * NB)
        ota = cut(2 * NH * NB)
        o_lat = cut(KVL)
        kmb = qb[:, 0:RH * RDK]
        PS = ctx.enter_context(nc.psum_tensor("PS", [P, 8 * 512], F32))
        bank = [PS[:, i * 512:(i + 1) * 512] for i in range(8)]

        const_in = sem("const_in")
        setup_in = sem("setup_in")
        zeroed = sem("zeroed")
        x_in = signal("x_in", 48)
        w_in_s = [signal(f"w_arrived{i}", 16 * (NBLK // WSLOTS)) for i in range(WSLOTS)]
        w_used = signal("w_used", NBLK)
        a_names = [("xT", 2), ("linA", NA), ("qlT", 1), ("ckT", 1), ("rqT", 1), ("rkT", 1), ("knat", 1), ("value", 1),
                   ("uq", 3), ("reto", 2), ("keyT", 2), ("qT", 2), ("probT", NH * (-(-T // 4))), ("rg", 4), ("bT", 2),
                   ("ob", 4), ("ovT", 1), ("oa", 2), ("gate", 8), ("mT", 2), ("x2T", 2), ("wq", 2 * PH * PD // BW),
                   ("pqT", 4)]
        blocks = set(first)
        A = Jobs(sem("act_filled"), sem("act_drained"), a_names,
                 bank[0:3 if sum(n for _, n in a_names) % 3 == 0 else 1], blocks, T)
        DJ = Jobs(sem("dve_filled"), sem("dve_drained"),
                 [("retA", 1), ("stateU", 1), ("score", NH), ("out", 2), ("pscore", 2)], [PS[:, 4 * 512:6 * 512]], blocks, T)
        KJ = Jobs(sem("keys_filled"), sem("keys_drained"), [("keys", 4)], bank[0:4], blocks)
        s_names = [("xT", 2), ("linA", NA), ("qlT", 1), ("ckT", 1), ("rqT", 1), ("uq", 3), ("qnT", 1), ("qrT", 1),
                   ("ukT", 4), ("qabs", 1), ("rg", 4), ("bT", 2), ("ob", 4), ("ovT", 1), ("oa", 2), ("gate", 8),
                   ("mT", 2), ("x2T", 2), ("wq", 2 * PH * PD // BW), ("pqT", 4)]
        AS = Jobs(sem("s_act_filled"), sem("s_act_drained"), s_names, bank[0:3], blocks, 1, A)
        DS = Jobs(sem("s_dve_filled"), sem("s_dve_drained"), [("out", 2), ("pscore", 2)], [PS[:, 4 * 512:6 * 512]],
                  blocks, 1, DJ)
        x_normed = signal("x_normed")
        lat_normed = signal("lat_normed")
        krope_ready = signal("krope_ready")
        ret_roped = signal("ret_roped")
        k_decayed = signal("k_decayed")
        q_roped = signal("q_roped")
        q_decayed = signal("q_decayed")
        keys_read = sem("keys_read")
        max_ready = signal("max_ready", NH)
        probs_ready = signal("probs_ready", NH)
        pv_done = signal("pv_done")
        heads_normed = signal("heads_normed")
        ret_negmean = signal("ret_negmean")
        ret_squares = signal("ret_squares")
        ret_rstd = signal("ret_rstd")
        ret_normed = signal("ret_normed", RH)
        ret_gated = signal("ret_gated")
        merged = signal("merged")
        x2_normed = signal("x2_normed")
        q_rstd_in = signal("q_rstd_in")
        top_shifted = signal("top_shifted")
        top_exp = signal("top_exp")
        chosen = signal("chosen")
        committed = signal("committed")
        ckv_stored = sem("ckv_stored")
        fd = Link(sem("front_steps"), "front", FRONT_LINKS)
        pdl = Link(sem("expert_steps"), "experts", EXPERT_LINKS)
        gate_pool, gate_dve, gate_pe, gate_sp = (sem(f"{e}_passed") for e in ("pool", "dve", "pe", "sp"))
        row_in = [sem(f"row_arrived{i}") for i in range(RING)]
        u_used = signal("u_used", P)
        v_used = signal("v_used", P)
        staged = sem("ids_staged")
        gelu_in = signal("gelu_in", PH)
        gelu_tanh = signal("gelu_tanh", PH)
        y_ready = signal("y_ready")
        y_stored = sem("y_stored")
        state_out = sem("state_out")
        table_in = sem("table_in")
        s_state_in = signal("s_state_in", 16)
        s_state_new = signal("s_state_new")
        s_state_stored = signal("s_state_stored", 16)
        s_masked = signal("s_masked", 2)
        s_outer = signal("s_outer")
        s_oret = signal("s_oret")
        s_oret_added = signal("s_oret_added")
        s_zero = sem("s_zero")
        s_ret_sum = sem("s_ret_sum")
        s_staged = signal("s_staged", 4)
        NCH = NPAGES // 4
        s_pages = [signal(f"s_pages{c}", 8 * 16) for c in range(NCH)]
        s_pv = signal("s_pv", NCH + 1)
        s_kt_filled = signal("s_kt_filled", 3 * NCH)
        s_kt_drained = signal("s_kt_drained", 3 * NCH)
        s_sc_filled = signal("s_sc_filled", NCH + 1)
        s_sc_drained = signal("s_sc_drained", NCH + 1)
        s_max = signal("s_max", NCH + 3)
        s_exp = signal("s_exp")
        s_prob = signal("s_prob", 2)
        s_pt_filled = signal("s_pt_filled", 2)
        s_pt_drained = signal("s_pt_drained", 2)
        s_ot_filled = signal("s_ot_filled")
        s_ot_drained = signal("s_ot_drained", 2)
        s_ov_filled = sem("s_ov_filled")

        block = ctx.enter_context(nc.Block())

        def sp_front(sp, t, sample=False):
            committed.wait(sp, t, 0)
            if sample:
                sp.wait_ge(s_zero, 1)
                sp.dma_start(xin[0:NB, :], a["x_sample"].rearrange("b s d -> (b s) d")).then_inc(x_in.sem, 16)
            else:
                sp.dma_start(xin[:, :], a["x_prompt"][0][ds(t * P, P), :]).then_inc(x_in.sem, 16)
            sp.dma_start(ropeb[:, :], const["rope"][ds(t * P, P), :]).then_inc(x_in.sem, 16)
            if not sample:
                sp.dma_start(maskb[:, 0:SEQ], const["mask"][:, ds((T - 1 - t) * P, SEQ)]).then_inc(x_in.sem, 16)

            def blocks(name):
                for n, (nm, w, c, wd) in enumerate(stream):
                    if nm != name:
                        continue
                    w_used.wait(sp, t, n + 1 - WSLOTS)
                    k = w.shape[0] // P
                    dst = wbuf[:, (n % WSLOTS) * KC * BW:(n % WSLOTS) * KC * BW + k * wd]
                    sp.dma_start(dst.rearrange("p (k c) -> p k c", k=k),
                                 w[:, c:c + wd].rearrange("(k p) c -> p k c", p=P)).then_inc(w_in_s[n % WSLOTS].sem, 16)

            blocks("linA")
            blocks("uq")
            krope_ready.wait(sp, t)
            if sample:
                sp.dma_start(out["ckv_s"].rearrange("l b s c -> (l b s) c"), z[0:NB, O_CKV:O_KR]).then_inc(ckv_stored, 16)
                sp.dma_start(out["krope_s"].rearrange("l b s c -> (l b s) c"), knat[0:NB, NOPE:HD]).then_inc(ckv_stored, 16)
            else:
                sp.dma_start(out["ckv_p"][0, 0].rearrange("n p c -> (n p) c")[ds(t * P, P), :],
                             z[:, O_CKV:O_KR]).then_inc(ckv_stored, 16)
                sp.dma_start(out["krope_p"][0, 0].rearrange("n p c -> (n p) c")[ds(t * P, P), :],
                             knat[:, NOPE:HD]).then_inc(ckv_stored, 16)
            if sample:
                sp_sample(sp)
            for name in ("rg", "ob", "oa", "gate", "out", "wq"):
                blocks(name)

        def sp_store_y(sp, t, n=P):
            y_ready.wait(sp, t)
            dst = (out["y_p"][0][ds(t * P, P), :] if n == P else out["y_s"].rearrange("b s d -> (b s) d"))
            sp.dma_start(dst, py[1][0:n, :]).then_inc(y_stored, 16)

        def s_state_buf(b):
            return KV[:, VAT + NPAGES * ROPE:VAT + NPAGES * ROPE + RH * RDV]

        def sp_sample(sp):
            pv_done.wait(sp, T - 1)

            def load_state(b):
                sp.dma_start(s_state_buf(b).rearrange("p (h e) -> p h e", h=RH),
                             a["state_ret"][0][ds(b, 1)].rearrange("o h d e -> d (o h) e")).then_inc(s_state_in.sem, 16)

            def load_pages(b, c):
                numbers = [sp.value_load(pages_reg[0:1, ds(b * NPAGES + 4 * c + k, 1)], min_val=0, max_val=NPHYS - 1)
                           for k in range(4)]
                for k, page in enumerate(numbers):
                    p = 4 * c + k
                    sp.dma_start(KV[:, p * KVL:(p + 1) * KVL],
                                 a["cache_ckv"][0][ds(page, 1)].rearrange("o p c -> (o p) c")).then_inc(s_pages[c].sem, 16)
                    sp.dma_start(KV[:, VAT + p * ROPE:VAT + (p + 1) * ROPE],
                                 a["cache_krope"][0][ds(page, 1)].rearrange("o p c -> (o p) c")).then_inc(s_pages[c].sem, 16)

            for b in range(NB):
                s_oret.wait(sp, b - 1)
                s_state_stored.wait(sp, b - 1)
                load_state(b)
                for c in range(NCH):
                    if c * NB // NCH == b:
                        load_pages(0, c)
                s_state_new.wait(sp, b)
                sp.dma_start(out["ret_s"][0][b:b + 1].rearrange("o h d e -> d (o h) e"),
                             s_state_buf(b).rearrange("p (h e) -> p h e", h=RH)).then_inc(s_state_stored.sem, 16)
            with sp.Fori(1, NB) as b:
                for c in range(NCH):
                    s_pv.wait(sp, b - 1, c + 1)
                    sp.sem_inc(gate_sp, 1)
                    load_pages(b, c)

        @block.sync
        def _(sp):
            n = 0
            for dst, src in ((ident[:, :], const["ident"]), (decay_t[:, :], const["decay"]), (q_decay[:, :], const["q_decay"]),
                             (k_decay[:, :], const["k_decay"]), (iota16[:, :], const["iota16"]), (diag8[:, :], const["diag8"]),
                             (ret_eye[:, :], const["ret_eye"]),
                             (ffn_gain[:, :], a["ffn_norm_g"].broadcast_to([P, D])),
                             (final_gain[:, :], a["final_norm_g"].rearrange("(a d) -> a d", a=1).broadcast_to([P, D])),
                             (kv_gain[:, :], a["kv_norm_g"].broadcast_to([P, KVL])),
                             (uk[:, :].rearrange("p (k c) -> p k c", k=2), a["w_uk"][0].rearrange("(k p) h n -> p k (h n)", p=P)),
                             (uv[:, :].rearrange("p (k c) -> p k c", k=2), a["w_uv"][0].rearrange("(k p) h n -> p k (h n)", p=P)),
                             ):
                sp.dma_start(dst, src).then_inc(const_in, 16)
                n += 16
            with nc.allow_non_contiguous_dma("gains are read once, one value per partition"):
                for dst, src in ((attn_gain_t, a["attn_norm_g"]), (q_gain_t, a["q_norm_g"]), (ret_gain_t, a["ret_norm_g"])):
                    sp.dma_start(dst[:, :], src[0].rearrange("(k p) -> p k", p=P)).then_inc(const_in, 16)
                    n += 16
            assert n == CONST_LOADS * 16
            sp.dma_start(rows[:, 0:2 * PH * PD].rearrange("p (g d) -> p g d", g=2 * PH),
                         a["peer_sub_keys"][0].rearrange("s h k d -> k (s h) d")).then_inc(setup_in, 16)
            sp.dma_start(pages_reg[0:1, :], a["page_table"].rearrange("(o b) n -> o (b n)", o=1)).then_inc(table_in, 16)
            sp.wait_ge(table_in, 16)
            sp_front(sp, 0)
            sp_front(sp, 1)
            sp_store_y(sp, 0)
            with sp.Fori(1, T - 1) as t:
                sp_front(sp, t + 1)
                sp_store_y(sp, t)
            sp_front(sp, T, sample=True)
            DJ.wait_drained(sp, T - 1, "stateU")
            sp.dma_start(out["ret_p"][0, 0].rearrange("h d e -> d h e"),
                         state[:, :].rearrange("p (h e) -> p h e", h=RH)).then_inc(state_out, 16)
            sp_store_y(sp, T - 1)
            sp_store_y(sp, T, NB)
            sp.wait_ge(state_out, 16)
            sp.wait_ge(y_stored, 16 * (T + 1))
            sp.wait_ge(ckv_stored, 32 * (T + 1))
            sp.wait_ge(s_state_stored.sem, 16 * NB)

        def pool_gathers(pool, t, h, s, n):
            for used, before, table in ((v_used, -TOPK, a["peer_u"][0]), (u_used, 0, a["peer_v"][0])):
                for k in range(TOPK):
                    slot = k % RING
                    if k >= RING:
                        prev, count = (u_used, h * TOPK + k + 1 - RING) if used is v_used else (v_used, h * TOPK + k + 1 - RING)
                    else:
                        prev, count = (v_used, (h - 1) * TOPK + k + 1 + TOPK - RING) if used is v_used else (u_used, h * TOPK + k + 1 + TOPK - RING)
                    value_ = t * P + count
                    if not isinstance(value_, int) or value_ > 0:
                        pool.wait_ge(prev.sem, value_)
                        pool.sem_inc(gate_pool, 1)
                    pool.indirect_dma_start(rows[0:n, slot * D:(slot + 1) * D], None, table,
                                            bass.IndirectOffsetOnAxis(ap=pe_id_s[s][0:n, k:k + 1], axis=0)
                                            ).then_inc(row_in[slot], 16)

        def pool_head(pool, t, h, s, n=P):
            value_ = t * P + (h - 1) * TOPK
            if not isinstance(value_, int) or value_ > 0:
                pool.wait_ge(v_used.sem, value_)
                pool.sem_inc(gate_pool, 1)
            nc.gpsimd.tensor_copy(pe_id_s[s][0:n, :], pe_id[0:n, ds(h * TOPK, TOPK)]).then_inc(staged, 1)
            pool.wait_ge(staged, t * PH + h + 1)
            pool.sem_inc(gate_pool, 1)
            pool_gathers(pool, t, h, s, n)

        @block.gpsimd
        def _(pool):
            nc.gpsimd.memset(KV[:, :], 0.0).then_inc(zeroed, 1)
            nc.gpsimd.memset(state[:, :], 0.0).then_inc(zeroed, 1)

            def tile(t, n=P, start=0):
                committed.wait(pool, t)
                pool.sem_inc(gate_pool, 1)
                if start:
                    for h in range(start):
                        pool_head(pool, t, h, h % 2, n)
                with pool.Fori(start // 2, PH // 2) as i:
                    pool_head(pool, t, 2 * i, 0, n)
                    pool_head(pool, t, 2 * i + 1, 1, n)

            pool.wait_ge(keys_read, 1)
            tile(0, start=2)
            with pool.Fori(1, T) as t:
                tile(t)
            tile(T, n=NB)

        def transposes(J, t, pe, name, i, chunks, n=P, m=P):
            J.may_fill(pe, t, name, i)
            b = J.bank(name, i)
            for k, src in enumerate(chunks):
                last = nc.tensor.transpose(b[0:m, k * n:(k + 1) * n], src, ident[0:n, 0:n])
            last.then_inc(J.filled, 1)

        def pe_block(pe, J, t, name, i, lhs, bnk=None, inc=True):
            n = first[name] + i
            _, w, _, wd = stream[n]
            k = w.shape[0] // P
            w_in_s[n % WSLOTS].wait(pe, t, 16 * (n // WSLOTS + 1))
            if bnk is None:
                J.may_fill(pe, t, name, i)
                bnk = J.bank(name, i)[:, 0:wd]
            base = (n % WSLOTS) * KC * BW
            for j in range(k):
                last = nc.tensor.matmul(bnk, lhs[:, j * P:(j + 1) * P], wbuf[:, base + j * wd:base + (j + 1) * wd],
                                        start=(j == 0), stop=(j == k - 1))
            last.then_inc(w_used.sem, 1)

        def pe_front(pe, t, sample=False):
            J, DD = (AS, DS) if sample else (A, DJ)
            tj = 0 if sample else t
            x_normed.wait(pe, t)
            for i in range(2):
                transposes(J, tj, pe, "xT", i, [sc[0][:, (4 * i + k) * P:(4 * i + k + 1) * P] for k in range(4)])
            J.wait_drained(pe, tj, "xT", 1)
            for i in range(NA):
                pe_block(pe, J, tj, "linA", i, xt) if not sample else pe_block_s(pe, J, t, "linA", i, xt)
            lat_normed.wait(pe, t)
            transposes(J, tj, pe, "qlT", 0, [z[:, k * P:(k + 1) * P] for k in range(QC)])
            transposes(J, tj, pe, "ckT", 0, [z[:, O_CKV + k * P:O_CKV + (k + 1) * P] for k in range(2)])
            ret_roped.wait(pe, t)
            transposes(J, tj, pe, "rqT", 0, [rqk[:, h * P:(h + 1) * P] for h in range(RH)])
            if not sample:
                transposes(J, tj, pe, "rkT", 0, [rqk[:, (RH + h) * P:(RH + h + 1) * P] for h in range(RH)])
                J.wait_drained(pe, tj, "ckT")
                for name, w in (("knat", uk), ("value", uv)):
                    J.may_fill(pe, tj, name)
                    for c in range(2):
                        last = nc.tensor.matmul(J.bank(name), t2[:, (3 + c) * P:(4 + c) * P], w[:, c * 512:(c + 1) * 512],
                                                start=(c == 0), stop=(c == 1))
                    last.then_inc(J.filled, 1)
            J.wait_drained(pe, tj, "qlT")
            for i in range(3):
                pe_block(pe, J, tj, "uq", i, t2) if not sample else pe_block_s(pe, J, t, "uq", i, t2)
            if sample:
                pe_sample(pe)
            else:
                J.wait_drained(pe, tj, "rkT")
                DD.may_fill(pe, tj, "retA")
                rb = DD.bank("retA")
                for h in range(RH):
                    last = nc.tensor.matmul(rb[:, h * P:(h + 1) * P], rkt[:, h * P:(h + 1) * P], rqt[:, h * P:(h + 1) * P],
                                            start=True, stop=True)
                last.then_inc(DD.filled, 1)
                DD.wait_drained(pe, tj, "retA")
                q_decayed.wait(pe, t)
                DD.wait_drained(pe, t - 1, "stateU")
                if isinstance(t, int) and t == 0:
                    pe.wait_ge(zeroed, 2)
                for i in range(2):
                    J.may_fill(pe, tj, "reto", i)
                    for h in (2 * i, 2 * i + 1):
                        o = J.bank("reto", i)[:, (h % 2) * RDV:(h % 2 + 1) * RDV]
                        nc.tensor.matmul(o, at[:, h * P:(h + 1) * P], z[:, O_RV + h * RDV:O_RV + (h + 1) * RDV],
                                         start=True, stop=False)
                        last = nc.tensor.matmul(o, rqd[:, h * P:(h + 1) * P], state[:, h * RDV:(h + 1) * RDV],
                                                start=False, stop=True)
                    last.then_inc(J.filled, 1)
                k_decayed.wait(pe, t)
                DD.may_fill(pe, tj, "stateU")
                for h in range(RH):
                    last = nc.tensor.matmul(DD.bank("stateU")[:, h * RDV:(h + 1) * RDV], kd[:, h * P:(h + 1) * P],
                                            z[:, O_RV + h * RDV:O_RV + (h + 1) * RDV], start=True, stop=True)
                last.then_inc(DD.filled, 1)
                krope_ready.wait(pe, t)
                J.wait_drained(pe, tj, "knat")
                for i in range(2):
                    transposes(J, tj, pe, "keyT", i, [knat[:, (4 * i + k) * HD:(4 * i + k + 1) * HD] for k in range(4)], m=HD)
                q_roped.wait(pe, t)
                for i in range(2):
                    transposes(J, tj, pe, "qT", i, [qb[:, (4 * i + k) * HD:(4 * i + k + 1) * HD] for k in range(4)], m=HD)
                J.wait_drained(pe, tj, "qT", 1)

                def scores(h):
                    DD.may_fill(pe, tj, "score", h)
                    for i in range(HALVES):
                        last = nc.tensor.matmul(DD.bank("score", h)[:, i * 512:i * 512 + HW], qt[0:HD, h * P:(h + 1) * P],
                                                key_t[0:HD, h, i * HW:(i + 1) * HW], start=True, stop=True)
                    last.then_inc(DD.filled, 1)

                NPT = -(-T // 4)
                scores(0)
                for h in range(NH):
                    if h + 1 < NH:
                        scores(h + 1)
                    probs_ready.wait(pe, t, h + 1)
                    for i in range(NPT):
                        transposes(J, tj, pe, "probT", NPT * h + i,
                                   [sc[h % 2][:, (4 * i + k) * P:(4 * i + k + 1) * P] for k in range(min(4, T - 4 * i))])
                    if h == 0:
                        heads_normed.wait(pe, t - 1)
                    for k in range(T):
                        if k % 4 == 0:
                            J.wait_drained(pe, tj, "probT", NPT * h + k // 4)
                        last = nc.tensor.matmul(bank[6][:, h * VH:(h + 1) * VH], pt[:, k * P:(k + 1) * P],
                                                value[:, k, h * VH:(h + 1) * VH], start=(k == 0), stop=(k == T - 1))
                last.then_inc(pv_done.sem, 1)
            blk = (lambda name, i, lhs, b=None: pe_block_s(pe, J, t, name, i, lhs, b)) if sample else \
                (lambda name, i, lhs, b=None: pe_block(pe, J, tj, name, i, lhs, b))
            for i in range(4):
                blk("rg", i, xt)
            ret_gated.wait(pe, t)
            for i in range(2):
                transposes(J, tj, pe, "bT", i, [oret[:, (4 * i + k) * P:(4 * i + k + 1) * P] for k in range(4)])
            J.wait_drained(pe, tj, "bT", 1)
            for i in range(4):
                blk("ob", i, t2)
            heads_normed.wait(pe, t)
            transposes(J, tj, pe, "ovT", 0, [qb[:, k * P:(k + 1) * P] for k in range(4)])
            J.wait_drained(pe, tj, "ovT")
            for i in range(2):
                blk("oa", i, t2)
            for i in range(8):
                blk("gate", i, xt)
            merged.wait(pe, t)
            for i in range(2):
                transposes(J, tj, pe, "mT", i, [oa[:, (4 * i + k) * P:(4 * i + k + 1) * P] for k in range(4)])
            J.wait_drained(pe, tj, "mT", 1)
            for i in range(4):
                if i % 2 == 0:
                    DD.may_fill(pe, tj, "out", i // 2)
                blk("out", i, t2, DD.bank("out")[:, (i % 2) * 256:(i % 2) * 256 + 256])
            x2_normed.wait(pe, t)
            for i in range(2):
                transposes(J, tj, pe, "x2T", i, [xn2[:, (4 * i + k) * P:(4 * i + k + 1) * P] for k in range(4)])
            J.wait_drained(pe, tj, "x2T", 1)
            for i in range(2 * PH * PD // BW):
                blk("wq", i, xt)
            J.wait_drained(pe, tj, "wq", 2 * PH * PD // BW - 1)
            for i in range(4):
                transposes(J, tj, pe, "pqT", i, [z[:, (4 * i + k) * P:(4 * i + k + 1) * P] for k in range(4)])
            for i in range(2):
                DD.may_fill(pe, tj, "pscore", i)
                for h in range(PH):
                    if h % 2 == 0:
                        J.wait_drained(pe, tj, "pqT", h // 2)
                    q, g = 2 * h + i, i * PH + h
                    last = nc.tensor.matmul(DD.bank("pscore", i)[:, h * P:(h + 1) * P], WK[:, q * P:(q + 1) * P],
                                            keys_t[:, g * P:(g + 1) * P], start=True, stop=True)
                last.then_inc(DD.filled, 1)

        def pe_block_s(pe, J, t, name, i, lhs, bnk=None):
            if bnk is None:
                J.may_fill(pe, 0, name, i)
                bnk = J.bank(name, i)[:, 0:stream[first[name] + i][3]]
            pe_block(pe, J, t, name, i, lhs, bnk)

        def pe_sample(pe):
            q_roped.wait(pe, T)
            AS.may_fill(pe, 0, "qnT")
            for h in range(NH):
                last = nc.tensor.transpose(AS.bank("qnT")[0:NOPE, h * NB:(h + 1) * NB], qb[0:NB, h * HD:h * HD + NOPE],
                                           ident[0:NB, 0:NB])
            last.then_inc(AS.filled, 1)
            AS.may_fill(pe, 0, "qrT")
            for h in range(NH):
                nc.tensor.transpose(AS.bank("qrT")[0:ROPE, h * NB:(h + 1) * NB], qb[0:NB, h * HD + NOPE:(h + 1) * HD],
                                    ident[0:NB, 0:NB])
            krope_ready.wait(pe, T)
            nc.tensor.transpose(AS.bank("qrT")[0:ROPE, NH * NB:(NH + 1) * NB], knat[0:NB, NOPE:HD],
                                ident[0:NB, 0:NB]).then_inc(AS.filled, 1)
            pe.wait_ge(DJ.drained, DJ.total)
            heads_normed.wait(pe, T - 1)

            def ret(b):
                s_masked.wait(pe, b)
                s_state_new.wait(pe, b, 0)
                for h in range(RH):
                    last = nc.tensor.matmul(PS[:, 4 * 512 + h * RDV:4 * 512 + (h + 1) * RDV], kmb[0:NB, h * P:(h + 1) * P],
                                            z[0:NB, O_RV + h * RDV:O_RV + (h + 1) * RDV], start=True, stop=True)
                last.then_inc(s_outer.sem, 1)
                s_state_new.wait(pe, b)
                s_oret_added.wait(pe, b, 0)
                for h in range(RH):
                    last = nc.tensor.matmul(PS[0:NB, 6 * 512 + h * RDV:6 * 512 + (h + 1) * RDV], qmb[:, h * NB:(h + 1) * NB],
                                            s_state_buf(b)[:, h * RDV:(h + 1) * RDV], start=True, stop=True)
                last.then_inc(s_oret.sem, 1)

            ret(0)
            with pe.Fori(1, NB) as b:
                ret(b)

            for i in range(4):
                AS.may_fill(pe, 0, "ukT", i)
                for k in range(4):
                    g = 4 * i + k
                    last = nc.tensor.transpose(AS.bank("ukT", i)[0:NOPE, k * P:(k + 1) * P],
                                               uk[:, (g % 2) * 512 + (g // 2) * NOPE:(g % 2) * 512 + (g // 2 + 1) * NOPE], ident[:, :])
                last.then_inc(AS.filled, 1)
            AS.wait_drained(pe, 0, "ukT", 3)
            AS.may_fill(pe, 0, "qabs")
            for g in range(2 * NH):
                last = nc.tensor.matmul(AS.bank("qabs")[:, ((g % 2) * NH + g // 2) * NB:((g % 2) * NH + g // 2 + 1) * NB],
                                        ukt[0:NOPE, g * P:(g + 1) * P],
                                        psq[0:NOPE, (g // 2) * NB:(g // 2 + 1) * NB], start=True, stop=True)
            last.then_inc(AS.filled, 1)

            AS.wait_drained(pe, 0, "qabs")
            s_oret_added.wait(pe, NB - 1)

            ktb = [KV[:, VAT + NPAGES * ROPE + i * 1536:VAT + NPAGES * ROPE + (i + 1) * 1536] for i in range(2)]

            def attend(b):
                s_staged.wait(pe, b)

                def turn(c):
                    s_pages[c].wait(pe, b)
                    for part in range(3):
                        s_kt_drained.wait(pe, b, 3 * c + part - 2)
                        w = P if part < 2 else ROPE
                        for k in range(4):
                            pg_ = 4 * c + k
                            src = KV[:, pg_ * KVL + part * P:pg_ * KVL + (part + 1) * P] if part < 2 else \
                                KV[:, VAT + pg_ * ROPE:VAT + (pg_ + 1) * ROPE]
                            last = nc.tensor.transpose(bank[part][0:w, k * P:(k + 1) * P], src, ident[:, :])
                        last.then_inc(s_kt_filled.sem, 1)

                def score(c):
                    s_kt_drained.wait(pe, b, 3 * c + 3)
                    s_sc_drained.wait(pe, b, c - 1)
                    for part in range(3):
                        w = P if part < 2 else ROPE
                        last = nc.tensor.matmul(bank[4 + c % 2][0:NH, :], qs[0:w, part * NH:(part + 1) * NH],
                                                ktb[c % 2][0:w, part * 512:(part + 1) * 512], start=(part == 0), stop=(part == 2))
                    last.then_inc(s_sc_filled.sem, 1)

                turn(0)
                for c in range(NCH):
                    if c + 1 < NCH:
                        turn(c + 1)
                    score(c)
                s_sc_drained.wait(pe, b, NCH - 1)
                for part in range(3):
                    w = P if part < 2 else ROPE
                    last = nc.tensor.matmul(bank[4 + NCH % 2][0:NH, 0:1], qs[0:w, part * NH:(part + 1) * NH],
                                            qs[0:w, 3 * NH + part:3 * NH + part + 1], start=(part == 0), stop=(part == 2))
                last.then_inc(s_sc_filled.sem, 1)
                s_exp.wait(pe, b)
                s_pt_drained.wait(pe, b, 0)
                pe.sem_inc(gate_pe, 1)
                for pg_ in range(NPAGES):
                    last = nc.tensor.transpose(bank[7][:, pg_ * NH:(pg_ + 1) * NH], WK[0:NH, pg_ * P:(pg_ + 1) * P],
                                               ident[0:NH, 0:NH])
                last.then_inc(s_pt_filled.sem, 1)
                s_prob.wait(pe, b, 2)
                pe.sem_inc(gate_pe, 1)
                nc.tensor.matmul(bank[3][0:NB, 448:448 + NH], psl[0:NH, 0:NB], ident[0:NH, 0:NH], start=True,
                                 stop=True).then_inc(s_pt_filled.sem, 1)
                s_pt_drained.wait(pe, b)
                s_ot_drained.wait(pe, b, 0)
                pe.sem_inc(gate_pe, 1)
                for pg_ in range(NPAGES):
                    last = nc.tensor.matmul(bank[6][0:NH, 0:KVL], ptb[:, pg_ * NH:(pg_ + 1) * NH],
                                            KV[:, pg_ * KVL:(pg_ + 1) * KVL], start=(pg_ == 0), stop=False)
                    if pg_ % 4 == 3:
                        last.then_inc(s_pv.sem, 1)
                nc.tensor.matmul(bank[6][0:NH, 0:KVL], psl[0:NB, NB:2 * NB], z[0:NB, O_CKV:O_KR], start=False,
                                 stop=True).then_inc(s_pv.sem, 1)
                s_ot_drained.wait(pe, b, 1)
                pe.sem_inc(gate_pe, 1)
                for c in range(2):
                    last = nc.tensor.transpose(bank[3][:, c * NH:(c + 1) * NH], o_lat[0:NH, c * P:(c + 1) * P],
                                               ident[0:NH, 0:NH])
                last.then_inc(s_ot_filled.sem, 1)

            attend(0)
            with pe.Fori(1, NB) as b:
                attend(b)
            s_ot_drained.wait(pe, NB - 1)
            for h in range(NH):
                for c in range(2):
                    last = nc.tensor.matmul(bank[6][0:NB, h * VH:(h + 1) * VH], ota[:, (c * NH + h) * NB:(c * NH + h + 1) * NB],
                                            uv[:, c * 512 + h * VH:c * 512 + (h + 1) * VH], start=(c == 0), stop=(c == 1))
            last.then_inc(s_ov_filled, 1)

        ukt = WK[:, 0:2 * NH * P]
        psq = rt

        @block.tensor
        def _(pe):
            pe.wait_ge(const_in, 16 * CONST_LOADS)
            pe.wait_ge(setup_in, 16)
            for i in range(4):
                transposes(KJ, 0, pe, "keys", i, [rows[:, (4 * i + k) * P:(4 * i + k + 1) * P] for k in range(4)])
            pe.wait_ge(KJ.drained, 4)
            pe.sem_inc(keys_read, 1)
            pe_front(pe, 0)
            pe_front(pe, 1)
            with pe.Fori(1, T - 1) as t:
                pe_front(pe, t + 1)
            pe_front(pe, T, sample=True)

        def act_block(act, J, t, tj, name, i, emit):
            w_used.wait(act, t, first[name] + i + 1)
            emit(J.bank(name, i)).then_inc(J.drained, 1)

        def act_drain(act, J, tj, name, i, emit):
            J.wait_filled(act, tj, name, i)
            emit(J.bank(name, i)).then_inc(J.drained, 1)

        copy = nc.scalar.copy

        def act_copy(dst, scale=1.0):
            return lambda b: nc.scalar.activation(dst, b, ACT.Copy, scale=scale)

        def act_front(act, t, sample=False):
            J = AS if sample else A
            tj = 0 if sample else t

            def gained(name, i, dst, gain, count=4):
                J.wait_filled(act, tj, name, i)
                b = J.bank(name, i)
                for k in range(count):
                    g = count * i + k
                    last = nc.scalar.activation(dst[:, g * P:(g + 1) * P], b[:, k * P:(k + 1) * P], ACT.Copy,
                                                scale=gain[:, g:g + 1])
                last.then_inc(J.drained, 1)

            for i in range(2):
                gained("xT", i, xt, attn_gain_t)
            yield "xT"
            for i in range(NA):
                wd = stream[i][3]
                act_block(act, J, t, tj, "linA", i, lambda b: nc.scalar.activation(z[:, i * BW:i * BW + wd], b[:, 0:wd], ACT.Copy))
                yield "lin"
            gained("qlT", 0, t2, q_gain_t, QC)
            act_drain(act, J, tj, "ckT", 0, lambda b: nc.scalar.activation(t2[:, 3 * P:5 * P], b[:, 0:2 * P], ACT.Copy))
            act_drain(act, J, tj, "rqT", 0, lambda b: nc.scalar.activation(rqt, b, ACT.Copy))
            if not sample:
                act_drain(act, J, tj, "rkT", 0, lambda b: nc.scalar.activation(rkt, b, ACT.Copy, scale=float(RDK) ** -0.5))
                act_drain(act, J, tj, "knat", 0, lambda b: nc.scalar.activation(
                    knat[:, :].rearrange("p (h d) -> p h d", h=NH)[:, :, 0:NOPE], b.rearrange("p (h d) -> p h d", h=NH), ACT.Copy))
                if isinstance(t, int) and t == 0:
                    act.wait_ge(zeroed, 2)
                act_drain(act, J, tj, "value", 0, lambda b: nc.scalar.activation(
                    KV[:, ds(t * (NH * VH) + VAT, NH * VH)], b, ACT.Copy))
            yield "lat"
            for i in range(3):
                act_block(act, J, t, tj, "uq", i, lambda b: nc.scalar.activation(qb[:, i * BW:(i + 1) * BW], b[:, 0:BW], ACT.Copy))
                yield "uq"
            if sample:
                act_sample(act)
                yield "reto"
            else:
                for i in range(2):
                    J.wait_filled(act, tj, "reto", i)
                    for h in (2 * i, 2 * i + 1):
                        last = nc.scalar.activation(oret[:, h * RDV:(h + 1) * RDV],
                                                    J.bank("reto", i)[:, (h % 2) * RDV:(h % 2 + 1) * RDV], ACT.Copy,
                                                    accum_out=rstat[:, h:h + 1])
                    last.then_inc(J.drained, 1)
                yield "reto"
            ret_negmean.wait(act, t)
            for h in range(RH):
                last = nc.scalar.activation(junk[:, h * RDV:(h + 1) * RDV],
                                            oret[:, h * RDV:(h + 1) * RDV], ACT.Square,
                                            bias=rstat[:, RH + h:RH + h + 1], accum_out=rstat[:, 2 * RH + h:2 * RH + h + 1])
            last.then_inc(ret_squares.sem, 1)
            yield "squares"
            ret_rstd.wait(act, t)
            for h in range(RH):
                nc.scalar.activation(oret[:, h * RDV:(h + 1) * RDV], oret[:, h * RDV:(h + 1) * RDV], ACT.Identity,
                                     bias=rstat[:, RH + h:RH + h + 1],
                                     scale=rstat[:, 3 * RH + h:3 * RH + h + 1]).then_inc(ret_normed.sem, 1)
            yield "normed"
            if sample:
                act_sample_attention(act)
                yield "keys"
            else:
                for i in range(2):
                    act_drain(act, J, tj, "keyT", i, lambda b: nc.scalar.activation(
                        KV[0:HD, 0:NH * SEQ].rearrange("p (h s) -> p h s", h=NH)[:, 4 * i:4 * i + 4, ds(t * P, P)],
                        b[0:HD, :].rearrange("p (h s) -> p h s", h=4), ACT.Copy))
                for i in range(2):
                    act_drain(act, J, tj, "qT", i, lambda b: nc.scalar.activation(qt[0:HD, 4 * i * P:4 * (i + 1) * P], b[0:HD, :], ACT.Copy))
                yield "keys"
                NPT = -(-T // 4)
                for h in range(NH):
                    max_ready.wait(act, t, h + 1)
                    nc.scalar.activation(sc[h % 2][:, 0:SEQ], sc[h % 2][:, 0:SEQ], ACT.Exp, bias=nmx[:, h:h + 1], scale=SCALE,
                                         accum_out=sums[:, h:h + 1]).then_inc(probs_ready.sem, 1)
                    for i in range(NPT):
                        w = min(4, T - 4 * i) * P
                        act_drain(act, J, tj, "probT", NPT * h + i,
                                  lambda b: nc.scalar.activation(pt[:, 4 * i * P:4 * i * P + w], b[:, 0:w], ACT.Copy))
                    yield "head"
            for i in range(4):
                w_used.wait(act, t, first["rg"] + i + 1)
                if i == 0:
                    heads_normed.wait(act, t)
                b = J.bank("rg", i)
                nc.scalar.activation(WK[:, i * BW:(i + 1) * BW], b[:, 0:BW], ACT.Tanh, scale=0.5)
                nc.scalar.activation(WK[:, D + i * BW:D + (i + 1) * BW], b[:, 0:BW], ACT.Copy).then_inc(J.drained, 1)
                yield "rg"
            for i in range(2):
                gained("bT", i, t2, ret_gain_t)
            for i in range(4):
                act_block(act, J, t, tj, "ob", i, lambda b: nc.scalar.activation(oret[:, i * BW:(i + 1) * BW], b[:, 0:BW], ACT.Copy))
                yield "ob"
            act_drain(act, J, tj, "ovT", 0, lambda b: nc.scalar.activation(t2[:, 0:512], b, ACT.Copy))
            for i in range(2):
                act_block(act, J, t, tj, "oa", i, lambda b: nc.scalar.activation(oa[:, i * 512:(i + 1) * 512], b, ACT.Copy))
                yield "oa"
            for i in range(8):
                act_block(act, J, t, tj, "gate", i, lambda b: nc.scalar.activation(WK[:, i * BW:(i + 1) * BW], b[:, 0:BW], ACT.Tanh, scale=0.5))
                yield "gate"
            for i in range(2):
                act_drain(act, J, tj, "mT", i, lambda b: nc.scalar.activation(t2[:, 4 * i * P:4 * (i + 1) * P], b, ACT.Copy, scale=0.5))
            yield "merge"
            yield "out"
            for i in range(2):
                act_drain(act, J, tj, "x2T", i, lambda b: nc.scalar.activation(xt[:, 4 * i * P:4 * (i + 1) * P], b, ACT.Copy))
            yield "x2"
            NQ = 2 * PH * PD // BW
            for i in range(NQ):
                w_used.wait(act, t, first["wq"] + i + 1)
                b = J.bank("wq", i)
                for k in range(2):
                    nc.scalar.activation(junk[:, (i % 4) * BW + k * P:(i % 4) * BW + (k + 1) * P], b[:, k * P:(k + 1) * P], ACT.Square,
                                         accum_out=ssq[:, 2 * i + k:2 * i + k + 1])
                nc.scalar.activation(z[:, i * BW:(i + 1) * BW], b[:, 0:BW], ACT.Copy).then_inc(J.drained, 1)
                yield "wq"
            for i in range(4):
                act_drain(act, J, tj, "pqT", i, lambda b: nc.scalar.activation(WK[:, 4 * i * P:4 * (i + 1) * P], b, ACT.Copy))
            yield "pqT"
            for _ in range(TOPK_YIELDS):
                yield "top"
            top_shifted.wait(act, t)
            nc.scalar.activation(gw[:, :], gw[:, :], ACT.Exp).then_inc(top_exp.sem, 1)
            yield "end"

        junk = WK[:, 3 * D:4 * D]

        def act_sample(act):
            act_drain(act, AS, 0, "qnT", 0, lambda b: nc.scalar.activation(psq[0:NOPE, 0:NH * NB], b[0:NOPE, 0:NH * NB], ACT.Copy))
            AS.wait_filled(act, 0, "qrT")
            nc.scalar.activation(nkr[0:ROPE, :], AS.bank("qrT")[0:ROPE, NH * NB:(NH + 1) * NB], ACT.Copy)
            nc.scalar.activation(qabs[0:ROPE, 2 * NH * NB:3 * NH * NB], AS.bank("qrT")[0:ROPE, 0:NH * NB],
                                 ACT.Copy).then_inc(AS.drained, 1)
            s_masked.wait(act, NB - 1)
            for i in range(4):
                act_drain(act, AS, 0, "ukT", i, lambda b: nc.scalar.activation(ukt[0:NOPE, 4 * i * P:4 * (i + 1) * P], b[0:NOPE, :], ACT.Copy))
            act_drain(act, AS, 0, "qabs", 0, lambda b: nc.scalar.activation(qabs[:, 0:2 * NH * NB], b[:, 0:2 * NH * NB], ACT.Copy))
            s_oret_added.wait(act, NB - 1)
            for h in range(RH):
                last = nc.scalar.activation(junk[:, h * RDV:(h + 1) * RDV], oret[:, h * RDV:(h + 1) * RDV], ACT.Copy,
                                            accum_out=rstat[:, h:h + 1])
            last.then_inc(s_ret_sum, 1)

        def act_sample_attention(act):
            AS.wait_drained(act, 0, "qabs")
            ktb = [KV[:, VAT + NPAGES * ROPE + i * 1536:VAT + NPAGES * ROPE + (i + 1) * 1536] for i in range(2)]
            s_state_stored.wait(act, NB - 1)

            def attend(b):
                s_sc_filled.wait(act, b, 0)
                nc.scalar.activation(qs[:, 0:2 * NH].rearrange("p (c h) -> p c h", c=2),
                                     qabs[:, 0:2 * NH * NB].rearrange("p (c h b) -> p c h b", c=2, h=NH)[:, :, :, ds(b, 1)]
                                     .rearrange("p c h b -> p c (h b)"), ACT.Copy).then_inc(s_staged.sem, 1)
                nc.scalar.activation(qs[0:ROPE, 2 * NH:3 * NH],
                                     qabs[0:ROPE, 2 * NH * NB:3 * NH * NB].rearrange("p (h b) -> p h b", h=NH)[:, :, ds(b, 1)]
                                     .rearrange("p h b -> p (h b)"), ACT.Copy).then_inc(s_staged.sem, 1)
                nc.scalar.activation(qs[:, 3 * NH:3 * NH + 2],
                                     t2[:, 3 * P:5 * P].rearrange("p (c b) -> p c b", c=2)[:, :, ds(b, 1)]
                                     .rearrange("p c b -> p (c b)"), ACT.Copy).then_inc(s_staged.sem, 1)
                nc.scalar.activation(qs[0:ROPE, 3 * NH + 2:3 * NH + 3], nkr[0:ROPE, ds(b, 1)], ACT.Copy).then_inc(s_staged.sem, 1)

                def keys(c):
                    for part in range(3):
                        w = P if part < 2 else ROPE
                        s_kt_filled.wait(act, b, 3 * c + part + 1)
                        if c >= 2 or part >= 0:
                            s_sc_filled.wait(act, b, c - 1)
                        nc.scalar.activation(ktb[c % 2][0:w, part * 512:(part + 1) * 512], bank[part][0:w, :],
                                             ACT.Copy).then_inc(s_kt_drained.sem, 1)

                def score(c):
                    s_sc_filled.wait(act, b, c + 1)
                    if c == 0:
                        s_pt_filled.wait(act, b, 0)
                    w = 512 if c < NCH else 1
                    nc.scalar.activation(WK[0:NH, c * 512:c * 512 + w], bank[4 + c % 2][0:NH, 0:w],
                                         ACT.Copy).then_inc(s_sc_drained.sem, 1)

                keys(0)
                for c in range(NCH):
                    if c + 1 < NCH:
                        keys(c + 1)
                    score(c)
                score(NCH)
                s_max.wait(act, b)
                nc.scalar.activation(WK[0:NH, 0:NPAGES * P + 1], WK[0:NH, 0:NPAGES * P + 1], ACT.Exp, bias=nmx[0:NH, 0:1],
                                     scale=SCALE, accum_out=sums[0:NH, 0:1]).then_inc(s_exp.sem, 1)
                s_pt_filled.wait(act, b, 1)
                s_pv.wait(act, b, 0)
                nc.scalar.activation(ptb[:, :], bank[7][:, 0:NPAGES * NH], ACT.Copy).then_inc(s_pt_drained.sem, 1)
                s_pt_filled.wait(act, b, 2)
                nc.scalar.activation(psl[0:NB, NB:2 * NB], bank[3][0:NB, 448:448 + NH], ACT.Copy).then_inc(s_pt_drained.sem, 1)
                s_pv.wait(act, b)
                s_ot_filled.wait(act, b, 0)
                nc.scalar.activation(o_lat[0:NH, :], bank[6][0:NH, 0:KVL], ACT.Copy,
                                     scale=sums[0:NH, 1:2]).then_inc(s_ot_drained.sem, 1)
                s_ot_filled.wait(act, b)
                nc.scalar.activation(ota[:, :].rearrange("p (c b) -> p c b", b=NB)[:, :, ds(b, 1)].rearrange("p c b -> p (c b)"),
                                     bank[3][:, 0:2 * NH], ACT.Copy).then_inc(s_ot_drained.sem, 1)

            attend(0)
            with act.Fori(1, NB) as b:
                attend(b)


        V = nc.vector

        def rsqrt(dve, link, x, n, tmp):
            y, u = tmp[:, 0:n], tmp[:, n:2 * n]
            link(dve, V.tensor_scalar(y.bitcast(I32), x.bitcast(I32), -0.5, RSQRT_MAGIC, ALU.mult, ALU.add))
            for _ in range(4):
                link(dve, V.tensor_tensor(u, y, y, ALU.mult))
                link(dve, V.tensor_tensor(u, u, x, ALU.mult))
                link(dve, V.tensor_scalar(u, u, -0.5, 1.5, ALU.mult, ALU.add))
                link(dve, V.tensor_tensor(y, y, u, ALU.mult))
            return y

        def spread(ap, n, width):
            return ap.unsqueeze(2).broadcast_to([P, n, width])

        def over(ap, n, width):
            return ap.unsqueeze(1).broadcast_to([P, n, width])

        def rotate(dve, link, src, dst, tmp_a, tmp_b, n, half, cos, nsin, sin):
            a4 = tmp_a.rearrange("p (n c d) -> p n c d", n=n, c=2)
            b4 = tmp_b.rearrange("p (n c d) -> p n c d", n=n, c=2)
            link.mark(V.tensor_tensor(a4[:, :, 0, :], src[:, :, 0:half], over(cos, n, half), ALU.mult))
            link.mark(V.tensor_tensor(a4[:, :, 1, :], src[:, :, half:2 * half], over(cos, n, half), ALU.mult))
            link.mark(V.tensor_tensor(b4[:, :, 0, :], src[:, :, half:2 * half], over(nsin, n, half), ALU.mult))
            link(dve, V.tensor_tensor(b4[:, :, 1, :], src[:, :, 0:half], over(sin, n, half), ALU.mult))
            return V.tensor_tensor(dst, tmp_a.rearrange("p (n d) -> p n d", n=n), tmp_b.rearrange("p (n d) -> p n d", n=n), ALU.add)

        RD2, MD2 = RDK // 2, ROPE // 2
        r_cos, r_nsin, r_sin = (ropeb[:, i * RD2:(i + 1) * RD2] for i in range(3))
        m_cos, m_nsin, m_sin = (ropeb[:, 3 * RD2 + i * MD2:3 * RD2 + (i + 1) * MD2] for i in range(3))

        def top16(dve, link, src, n, width, vals, idx):
            def every(f):
                dve.sem_inc(gate_dve, 1)
                for g in range(n):
                    link.mark(f(g, src[:, g * width:(g + 1) * width], slice(g * TOPK, g * TOPK + 8), slice(g * TOPK + 8, (g + 1) * TOPK)))
                link.join(dve)
            every(lambda g, s, lo, hi: V.max(vals[:, lo], s))
            yield "top"
            every(lambda g, s, lo, hi: V.max_index(idx[:, lo], vals[:, lo], s))
            yield "top"
            every(lambda g, s, lo, hi: V.match_replace(s, vals[:, lo], s, NEG))
            yield "top"
            every(lambda g, s, lo, hi: V.max(vals[:, hi], s))
            yield "top"
            every(lambda g, s, lo, hi: V.max_index(idx[:, hi], vals[:, hi], s))
            yield "top"

        def dve_front(dve, t, sample=False):
            J, DD = (AS, DS) if sample else (A, DJ)
            tj = 0 if sample else t
            link = fd
            link.begin(t)
            if sample:
                dve.wait_ge(x_in.sem, 48 * T + 32)
            else:
                x_in.wait(dve, t)
            link(dve, V.tensor_tensor_reduce(out=sc[0], in0=xin[:, :], in1=xin[:, :], scale=1.0, scalar=0.0, op0=ALU.mult,
                                             op1=ALU.add, accum_out=stat[:, 0:1]))
            link(dve, V.tensor_scalar(stat[:, 0:1], stat[:, 0:1], 1.0 / D, EPS, ALU.mult, ALU.add))
            r = rsqrt(dve, link, stat[:, 0:1], 1, nr)
            V.tensor_scalar(sc[0], xin[:, :], r, None, ALU.mult).then_inc(x_normed.sem, 1)
            yield "xT"
            for i in range(NA):
                yield "lin"
            J.wait_drained(dve, tj, "linA", NA - 1)
            x_normed.wait(dve, t)
            link.mark(V.tensor_tensor_reduce(out=rt[:, 0:QL], in0=z[:, 0:QL], in1=z[:, 0:QL], scale=1.0, scalar=0.0,
                                             op0=ALU.mult, op1=ALU.add, accum_out=stat[:, 1:2]))
            link(dve, V.tensor_tensor_reduce(out=knat[:, 0:KVL], in0=z[:, O_CKV:O_KR], in1=z[:, O_CKV:O_KR], scale=1.0,
                                             scalar=0.0, op0=ALU.mult, op1=ALU.add, accum_out=stat[:, 2:3]))
            link.mark(V.tensor_scalar(stat[:, 1:2], stat[:, 1:2], 1.0 / QL, EPS, ALU.mult, ALU.add))
            link(dve, V.tensor_scalar(stat[:, 2:3], stat[:, 2:3], 1.0 / KVL, EPS, ALU.mult, ALU.add))
            r = rsqrt(dve, link, stat[:, 1:3], 2, nr)
            link.mark(V.tensor_scalar(z[:, 0:QL], z[:, 0:QL], r[:, 0:1], None, ALU.mult))
            V.scalar_tensor_tensor(out=z[:, O_CKV:O_KR], in0=z[:, O_CKV:O_KR], scalar=r[:, 1:2], in1=kv_gain[:, :],
                                   op0=ALU.mult, op1=ALU.mult).then_inc(lat_normed.sem, 1)
            kr = z[:, O_KR:O_RQ].unsqueeze(1)
            ra = rt[:, 0:ROPE]
            rb = rt[:, ROPE:2 * ROPE]
            link.mark(V.tensor_tensor(ra[:, 0:MD2], z[:, O_KR:O_KR + MD2], m_cos, ALU.mult))
            link.mark(V.tensor_tensor(ra[:, MD2:ROPE], z[:, O_KR + MD2:O_RQ], m_cos, ALU.mult))
            link.mark(V.tensor_tensor(rb[:, 0:MD2], z[:, O_KR + MD2:O_RQ], m_nsin, ALU.mult))
            link(dve, V.tensor_tensor(rb[:, MD2:ROPE], z[:, O_KR:O_KR + MD2], m_sin, ALU.mult))
            V.tensor_tensor(knat[:, :].rearrange("p (h d) -> p h d", h=NH)[:, :, NOPE:HD], over(ra, NH, ROPE),
                            over(rb, NH, ROPE), ALU.add).then_inc(krope_ready.sem, 1)
            rotate(dve, link, z[:, O_RQ:O_RV].rearrange("p (n d) -> p n d", n=2 * RH),
                   rqk.rearrange("p (n d) -> p n d", n=2 * RH), rqk, WK[:, 0:D], 2 * RH, RD2, r_cos, r_nsin, r_sin
                   ).then_inc(ret_roped.sem, 1)
            ret_roped.wait(dve, t)
            if not sample:
                V.tensor_tensor(kd.rearrange("p (h d) -> p h d", h=RH), rqk[:, RH * P:].rearrange("p (h d) -> p h d", h=RH),
                                spread(k_decay[:, :], RH, P), ALU.mult).then_inc(k_decayed.sem, 1)
            yield "lat"
            for i in range(3):
                yield "uq"
            J.wait_drained(dve, tj, "uq", 2)
            krope_ready.wait(dve, t)
            q3 = qb[:, :].rearrange("p (h d) -> p h d", h=NH)[:, :, NOPE:HD]
            rotate(dve, link, q3, q3, rt[:, 0:NH * ROPE], rt[:, NH * ROPE:2 * NH * ROPE], NH, MD2, m_cos, m_nsin, m_sin
                   ).then_inc(q_roped.sem, 1)
            if sample:
                dve_sample_ret(dve)
                dve.wait_ge(s_ret_sum, 1)
            else:
                J.wait_drained(dve, tj, "rqT")
                V.tensor_tensor(rqd, rqt, q_decay[:, :], ALU.mult).then_inc(q_decayed.sem, 1)
                DD.wait_filled(dve, tj, "retA")
                k_decayed.wait(dve, t)
                V.tensor_tensor(at, DD.bank("retA")[:, 0:512], decay_t[:, :], ALU.mult).then_inc(DD.drained, 1)
                DD.wait_filled(dve, tj, "stateU")
                if isinstance(t, int) and t == 0:
                    dve.wait_ge(zeroed, 2)
                for h in range(RH):
                    hs = slice(h * RDV, (h + 1) * RDV)
                    ins = V.scalar_tensor_tensor(out=state[:, hs], in0=state[:, hs], scalar=const["chunk_decay"][h],
                                                 in1=DD.bank("stateU")[:, hs], op0=ALU.mult, op1=ALU.add)
                    if h < RH - 1:
                        link.mark(ins)
                ins.then_inc(DD.drained, 1)
                J.wait_drained(dve, tj, "reto", 1)
            V.tensor_scalar(rstat[:, RH:2 * RH], rstat[:, 0:RH], -1.0 / RDV, None, ALU.mult).then_inc(ret_negmean.sem, 1)
            yield "reto"
            ret_squares.wait(dve, t)
            link(dve, V.tensor_scalar(rstat[:, 2 * RH:3 * RH], rstat[:, 2 * RH:3 * RH], 1.0 / RDV, EPS, ALU.mult, ALU.add))
            r = rsqrt(dve, link, rstat[:, 2 * RH:3 * RH], RH, nr)
            link(dve, V.tensor_copy(rstat[:, 3 * RH:4 * RH], r))
            V.tensor_tensor(rstat[:, RH:2 * RH], rstat[:, RH:2 * RH], r, ALU.mult).then_inc(ret_rstd.sem, 1)
            yield "squares"
            yield "normed"
            if sample:
                dve_sample(dve)
            yield "keys"
            if not sample:
                for h in range(NH):
                    DD.wait_filled(dve, tj, "score", h)
                    if h == 0:
                        ret_normed.wait(dve, t)
                    if h >= 2:
                        A_job_read(dve, t, h - 2)
                    dve.sem_inc(gate_dve, 1)
                    V.tensor_tensor_reduce(out=sc[h % 2][:, 0:SEQ], in0=DD.bank("score", h)[:, 0:SEQ], in1=maskb[:, 0:SEQ],
                                           scale=1.0, scalar=NEG * 2, op0=ALU.add, op1=ALU.max,
                                           accum_out=mx[:, h:h + 1]).then_inc(DD.drained, 1)
                    DD.wait_drained(dve, tj, "score", h)
                    V.tensor_scalar(nmx[:, h:h + 1], mx[:, h:h + 1], -SCALE, None, ALU.mult).then_inc(max_ready.sem, 1)
                    yield "head"
                probs_ready.wait(dve, t)
                link(dve, V.reciprocal(sums[:, :], sums[:, :]))
                pv_done.wait(dve, t)
                V.tensor_tensor(qb[:, 0:NH * VH].rearrange("p (h d) -> p h d", h=NH),
                                bank[6].rearrange("p (h d) -> p h d", h=NH), spread(sums[:, :], NH, VH),
                                ALU.mult).then_inc(heads_normed.sem, 1)
            for i in range(4):
                yield "rg"
            J.wait_drained(dve, tj, "rg", 3)
            ret_normed.wait(dve, t)
            link(dve, V.scalar_tensor_tensor(out=WK[:, D:2 * D], in0=WK[:, 0:D], scalar=1.0, in1=WK[:, D:2 * D], op0=ALU.add,
                                             op1=ALU.mult))
            V.scalar_tensor_tensor(out=oret[:, :], in0=WK[:, D:2 * D], scalar=0.5, in1=oret[:, :], op0=ALU.mult,
                                   op1=ALU.mult).then_inc(ret_gated.sem, 1)
            for name in ["ob"] * 4 + ["oa"] * 2 + ["gate"] * 8:
                yield name
            J.wait_drained(dve, tj, "gate", 7)
            link.mark(V.scalar_tensor_tensor(out=oa, in0=WK[:, 0:D], scalar=1.0, in1=oa, op0=ALU.add, op1=ALU.mult))
            link(dve, V.scalar_tensor_tensor(out=oret[:, :], in0=WK[:, D:2 * D], scalar=1.0, in1=oret[:, :], op0=ALU.add, op1=ALU.mult))
            V.tensor_tensor(oa, oa, oret[:, :], ALU.add).then_inc(merged.sem, 1)
            yield "merge"
            for i in range(2):
                w_used.wait(dve, t, first["out"] + 2 * i + 2)
                V.tensor_tensor(xin[:, i * 512:(i + 1) * 512], DD.bank("out")[:, 0:512], xin[:, i * 512:(i + 1) * 512],
                                ALU.add).then_inc(DD.drained, 1)
            yield "out"
            DD.wait_drained(dve, tj, "out", 1)
            link(dve, V.tensor_tensor_reduce(out=WK[:, 0:D], in0=xin[:, :], in1=xin[:, :], scale=1.0, scalar=0.0, op0=ALU.mult,
                                             op1=ALU.add, accum_out=stat[:, 3:4]))
            link(dve, V.tensor_scalar(stat[:, 3:4], stat[:, 3:4], 1.0 / D, EPS, ALU.mult, ALU.add))
            r = rsqrt(dve, link, stat[:, 3:4], 1, nr)
            V.scalar_tensor_tensor(out=xn2, in0=xin[:, :], scalar=r, in1=ffn_gain[:, :], op0=ALU.mult,
                                   op1=ALU.mult).then_inc(x2_normed.sem, 1)
            yield "x2"
            for i in range(2 * PH * PD // BW):
                yield "wq"
            J.wait_drained(dve, tj, "wq", 2 * PH * PD // BW - 1)
            x2_normed.wait(dve, t)
            link(dve, V.tensor_scalar(ssq[:, :], ssq[:, :], 1.0 / PD, EPS, ALU.mult, ALU.add))
            r = rsqrt(dve, link, ssq[:, :], 2 * PH, nr)
            yield "pqT"
            for i in range(2):
                DD.wait_filled(dve, tj, "pscore", i)
                V.tensor_tensor(z[:, i * D:(i + 1) * D].rearrange("p (g k) -> p g k", g=PH),
                                DD.bank("pscore", i).rearrange("p (g k) -> p g k", g=PH),
                                spread(r[:, i:2 * PH:2], PH, P), ALU.mult).then_inc(DD.drained, 1)
            DD.wait_drained(dve, tj, "pscore", 1)
            yield from top16(dve, link, z, 2 * PH, P, sv, si)
            link.mark(V.tensor_copy(sif[:, :], si[:, :]))
            cand = z[:, 0:PH * 256]
            for h in range(PH):
                c3 = cand[:, h * 256:(h + 1) * 256].rearrange("p (a b) -> p a b", a=TOPK)
                link.mark(V.tensor_tensor(c3, spread(sv[:, h * TOPK:(h + 1) * TOPK], TOPK, TOPK),
                                          over(sv[:, (PH + h) * TOPK:(PH + h + 1) * TOPK], TOPK, TOPK), ALU.add))
            link.join(dve)
            yield "top"
            yield from top16(dve, link, cand, PH, 256, ts_, tp)
            V.tensor_tensor(gw[:, :].rearrange("p (h k) -> p h k", h=PH), ts_[:, :].rearrange("p (h k) -> p h k", h=PH),
                            ts_[:, :].rearrange("p (h k) -> p h k", h=PH)[:, :, 0:1].broadcast_to([P, PH, TOPK]),
                            ALU.subtract).then_inc(top_shifted.sem, 1)
            for which, (op, arg, dst) in enumerate(((ALU.logical_shift_right, 4, i0), (ALU.bitwise_and, 15, i1))):
                link(dve, V.tensor_scalar(tq[:, :], tp[:, :], arg, None, op))
                link(dve, V.tensor_copy(tf[:, :], tq[:, :]))
                oh = WK[:, 0:P * TOPK]
                link(dve, V.tensor_tensor(oh.rearrange("p (s a) -> p s a", s=P), spread(tf[:, :], P, TOPK),
                                          over(iota16[:, :], P, TOPK), ALU.is_equal))
                for h in range(PH):
                    o3 = oh[:, h * 256:(h + 1) * 256].rearrange("p (k a) -> p k a", k=TOPK)
                    link.mark(V.tensor_tensor(o3, o3, over(sif[:, (which * PH + h) * TOPK:(which * PH + h + 1) * TOPK], TOPK, TOPK), ALU.mult))
                link.join(dve)
                link(dve, V.tensor_reduce(dst[:, :], oh.rearrange("p (s a) -> p s a", s=P), AX, ALU.add))
                yield "top"
            link(dve, V.scalar_tensor_tensor(out=i0[:, :], in0=i0[:, :], scalar=float(NK), in1=i1[:, :], op0=ALU.mult, op1=ALU.add))
            link.mark(V.tensor_copy(eid[:, :], i0[:, :]))
            top_exp.wait(dve, t)
            link(dve, V.tensor_reduce(gs[:, 0:PH], gw[:, :].rearrange("p (h k) -> p h k", h=PH), AX, ALU.add))
            link(dve, V.reciprocal(gs[:, PH:2 * PH], gs[:, 0:PH]))
            V.tensor_tensor(gw[:, :].rearrange("p (h k) -> p h k", h=PH), gw[:, :].rearrange("p (h k) -> p h k", h=PH),
                            spread(gs[:, PH:2 * PH], PH, TOPK), ALU.mult).then_inc(chosen.sem, 1)
            if not sample:
                link.end()
            yield "end"

        def A_job_read(dve, t, h):
            NPT = -(-T // 4)
            A.wait_filled(dve, t, "probT", NPT * (h + 1) - 1)

        def dve_sample_ret(dve):
            AS.wait_drained(dve, 0, "rqT")
            dve.wait_ge(s_zero, 2)

            def one(b):
                s_outer.wait(dve, b, 0)
                s_oret.wait(dve, b, 0)
                V.tensor_scalar(kmb[0:NB, :], rqk[0:NB, RH * P:2 * RH * P], ret_eye[0:NB, ds(b, 1)], None,
                                ALU.mult).then_inc(s_masked.sem, 1)
                V.tensor_tensor(qmb[:, :].rearrange("p (h b) -> p h b", h=RH),
                                rqt.rearrange("p (h c) -> p h c", h=RH)[:, :, 0:NB],
                                diag8[:, ds(b * NB, NB)].unsqueeze(1).broadcast_to([P, RH, NB]), ALU.mult).then_inc(s_masked.sem, 1)
                s_state_in.wait(dve, b)
                s_outer.wait(dve, b)
                for h in range(RH):
                    hs = slice(h * RDV, (h + 1) * RDV)
                    last = V.scalar_tensor_tensor(out=s_state_buf(b)[:, hs], in0=s_state_buf(b)[:, hs], scalar=const["gamma"][h],
                                                  in1=PS[:, 4 * 512 + h * RDV:4 * 512 + (h + 1) * RDV], op0=ALU.mult, op1=ALU.add)
                last.then_inc(s_state_new.sem, 1)
                s_oret.wait(dve, b)
                s_oret_added.wait(dve, b, 0)
                V.tensor_tensor(oret[0:NB, :], oret[0:NB, :], PS[0:NB, 6 * 512:6 * 512 + D], ALU.add).then_inc(s_oret_added.sem, 1)

            q_kmb_free(dve)
            one(0)
            with dve.Fori(1, NB) as b:
                one(b)

        def q_kmb_free(dve):
            AS.wait_drained(dve, 0, "qrT")

        def dve_sample(dve):
            def one(b):
                for c in range(NCH + 1):
                    s_sc_drained.wait(dve, b, c + 1)
                    w = 512 if c < NCH else 1
                    V.tensor_reduce(nr[0:NH, c:c + 1], WK[0:NH, c * 512:c * 512 + w], AX, ALU.max).then_inc(s_max.sem, 1)
                s_max.wait(dve, b, NCH + 1)
                V.tensor_reduce(mx[0:NH, 0:1], nr[0:NH, 0:NCH + 1], AX, ALU.max).then_inc(s_max.sem, 1)
                s_max.wait(dve, b, NCH + 2)
                V.tensor_scalar(nmx[0:NH, 0:1], mx[0:NH, 0:1], -SCALE, None, ALU.mult).then_inc(s_max.sem, 1)
                s_exp.wait(dve, b)
                s_ot_drained.wait(dve, b, 0)
                V.tensor_scalar(psl[0:NH, 0:NB], diag8[0:NH, ds(b * NB, NB)], WK[0:NH, NPAGES * P:NPAGES * P + 1], None,
                                ALU.mult).then_inc(s_prob.sem, 1)
                V.reciprocal(sums[0:NH, 1:2], sums[0:NH, 0:1]).then_inc(s_prob.sem, 1)

            one(0)
            with dve.Fori(1, NB) as b:
                one(b)
            dve.wait_ge(s_ov_filled, 1)
            AS.wait_drained(dve, 0, "qrT")
            V.memset(qb[:, :], 0.0).then_inc(s_zero, 1)
            dve.wait_ge(s_zero, 3)
            V.tensor_copy(qb[0:NB, 0:NH * VH], bank[6][0:NB, :]).then_inc(heads_normed.sem, 1)


        def dve_experts(dve, t, n=P):
            link = pdl
            link.t, link.k = t, 3
            for h in range(PH):
                for q in range(4):
                    for k in range(4 * q, 4 * q + 4):
                        slot = k % RING
                        dve.wait_ge(row_in[slot], (t * PH + h) * (2 * TOPK // RING) * 16 + (k // RING + 1) * 16)
                        if h == 0 and k == 0:
                            committed.wait(dve, t)
                        row = rows[0:n, slot * D:(slot + 1) * D]
                        V.tensor_tensor_reduce(out=row, in0=row, in1=px[0:n, :], scale=1.0, scalar=0.0, op0=ALU.mult,
                                               op1=ALU.add, accum_out=dots[0:n, k:k + 1]).then_inc(u_used.sem, 1)
                    yield "u"
                u_used.wait(dve, t, (h + 1) * TOPK)
                link(dve, V.tensor_tensor(ga_[0:n, :], dots[0:n, :], dots[0:n, :], ALU.mult))
                link(dve, V.tensor_scalar(ga_[0:n, :], ga_[0:n, :], GELU_A, 1.0, ALU.mult, ALU.add))
                V.tensor_tensor(ga_[0:n, :], ga_[0:n, :], dots[0:n, :], ALU.mult).then_inc(gelu_in.sem, 1)
                gelu_tanh.wait(dve, t, h + 1)
                link(dve, V.scalar_tensor_tensor(out=ga_[0:n, :], in0=gb_[0:n, :], scalar=1.0, in1=dots[0:n, :], op0=ALU.add, op1=ALU.mult))
                v_used.wait(dve, t, h * TOPK)
                link(dve, V.scalar_tensor_tensor(out=gcoef[0:n, :], in0=ga_[0:n, :], scalar=0.5, in1=pg[0:n, h * TOPK:(h + 1) * TOPK],
                                                 op0=ALU.mult, op1=ALU.mult))
                yield "gelu"
                for q in range(4):
                    for k in range(4 * q, 4 * q + 4):
                        slot = k % RING
                        dve.wait_ge(row_in[slot], (t * PH + h) * (2 * TOPK // RING) * 16 + (TOPK // RING + k // RING + 1) * 16)
                        row = rows[0:n, slot * D:(slot + 1) * D]
                        y = py[k % 2][0:n, :]
                        if h == 0 and k == 1:
                            value_ = t * 16
                            if not isinstance(t, int) or t > 0:
                                dve.wait_ge(y_stored, value_)
                            V.tensor_scalar(y, row, gcoef[0:n, k:k + 1], None, ALU.mult).then_inc(v_used.sem, 1)
                            continue
                        v_used.wait(dve, t, h * TOPK + k - 1)
                        V.scalar_tensor_tensor(out=y, in0=row, scalar=gcoef[0:n, k:k + 1], in1=y, op0=ALU.mult,
                                               op1=ALU.add).then_inc(v_used.sem, 1)
                    yield "v"
            v_used.wait(dve, t, P)
            link(dve, V.tensor_tensor(py[0][0:n, :], py[0][0:n, :], py[1][0:n, :], ALU.add))
            link(dve, V.tensor_tensor_reduce(out=py[1][0:n, :], in0=py[0][0:n, :], in1=py[0][0:n, :], scale=1.0, scalar=0.0,
                                             op0=ALU.mult, op1=ALU.add, accum_out=fin[0:n, 0:1]))
            link(dve, V.tensor_scalar(fin[0:n, 0:1], fin[0:n, 0:1], 1.0 / D, EPS, ALU.mult, ALU.add))
            r = rsqrt(dve, link, fin[0:n, 0:1], 1, fin[0:n, 2:4])
            V.scalar_tensor_tensor(out=py[1][0:n, :], in0=py[0][0:n, :], scalar=r, in1=final_gain[0:n, :], op0=ALU.mult,
                                   op1=ALU.mult).then_inc(y_ready.sem, 1)
            pdl.end()
            yield "fin"

        def dve_commit(dve, t):
            pdl.begin(t)
            chosen.wait(dve, t)
            y_ready.wait(dve, t - 1)
            pdl.mark(V.tensor_copy(pe_id[:, :], eid[:, :]))
            pdl.mark(V.tensor_copy(pg[:, :], gw[:, :]))
            pdl.mark(V.tensor_copy(px[:, :], xn2))
            V.tensor_copy(py[0][:, :], xin[:, :]).then_inc(committed.sem, 1)
            committed.wait(dve, t)

        def act_experts(act, t, n=P):
            for h in range(PH):
                for _ in range(4):
                    yield "u"
                gelu_in.wait(act, t, h + 1)
                nc.scalar.activation(gb_[0:n, :], ga_[0:n, :], ACT.Tanh, scale=GELU_C).then_inc(gelu_tanh.sem, 1)
                yield "gelu"
                for _ in range(4):
                    yield "v"
            yield "fin"

        checkpoints = []

        def beside(front, experts):
            checkpoints.append([(at_, next(experts, None)) for at_ in front] + list(experts))

        @block.scalar
        def _(act):
            act.wait_ge(const_in, 16 * CONST_LOADS)
            for i in range(4):
                KJ.wait_filled(act, 0, "keys", i)
                nc.scalar.activation(keys_t[:, 4 * i * P:4 * (i + 1) * P], KJ.bank("keys", i), ACT.Copy).then_inc(KJ.drained, 1)
            for _ in act_front(act, 0):
                pass
            beside(act_front(act, 1), act_experts(act, 0))
            with act.Fori(1, T - 1) as t:
                beside(act_front(act, t + 1), act_experts(act, t))
            beside(act_front(act, T, sample=True), act_experts(act, T - 1))
            for _ in act_experts(act, T, NB):
                pass

        @block.vector
        def _(dve):
            dve.wait_ge(const_in, 16 * CONST_LOADS)
            for _ in dve_front(dve, 0):
                pass
            dve_commit(dve, 0)
            beside(dve_front(dve, 1), dve_experts(dve, 0))
            dve_commit(dve, 1)
            with dve.Fori(1, T - 1) as t:
                beside(dve_front(dve, t + 1), dve_experts(dve, t))
                dve_commit(dve, t + 1)
            V.memset(xin[:, :], 0.0).then_inc(s_zero, 1)
            x2_normed.wait(dve, T - 1)
            V.memset(oret[:, :], 0.0).then_inc(s_zero, 1)
            beside(dve_front(dve, T, sample=True), dve_experts(dve, T - 1))
            dve_commit(dve, T)
            for _ in dve_experts(dve, T, NB):
                pass

        half = len(checkpoints) // 2
        assert checkpoints[:half] == checkpoints[half:]


FRONT_LINKS = 273
EXPERT_LINKS = 55
CONST_LOADS = 15
TOPK_YIELDS = 13


_INS = ['x_prompt', 'x_sample', 'cache_ckv', 'cache_krope', 'state_ret', 'page_table', 'attn_norm_g', 'w_in', 'q_norm_g',
        'w_uq', 'kv_norm_g', 'w_uk', 'w_uv', 'ret_norm_g', 'w_oa', 'w_ob', 'w_out', 'ffn_norm_g', 'peer_w_q',
        'peer_sub_keys', 'peer_u', 'peer_v', 'final_norm_g']


def _constants(seq, past, rope, rdk, rh, nb):
    f = np.float32
    t = seq // P
    pos = np.concatenate([np.arange(seq), np.full(P, past)]).astype(f)

    def angles(d):
        inv = (f(ROPE_BASE) ** (-np.arange(0, d, 2, dtype=f) / f(d))).astype(f)
        ang = (pos[:, None] * inv[None, :]).astype(f).astype(np.float64)
        return [np.cos(ang), -np.sin(ang), np.sin(ang)]

    lg = np.log1p(-np.exp2(-5.0 - np.arange(rh, dtype=f)).astype(f)).astype(np.float64)
    i = np.arange(P)
    rel = i[None, :] - i[:, None]
    decay = np.where(rel[:, None, :] >= 0, np.exp(np.maximum(rel, 0)[:, None, :] * lg[None, :, None]), 0.0)
    q_decay = np.broadcast_to(np.exp((i[None, :] + 1.0) * lg[:, None])[None], (P, rh, P))
    k_decay = np.exp((P - 1.0 - i)[:, None] * lg[None, :]) * float(rdk) ** -0.5
    u = np.arange(2 * seq - P)
    mask = np.where(u[None, :] <= (seq - P) + i[:, None], 0.0, NEG)
    tables = {
        "ident": np.eye(P), "rope": np.concatenate(angles(rdk) + angles(rope), 1), "mask": mask,
        "decay": decay.reshape(P, -1), "q_decay": q_decay.reshape(P, -1), "k_decay": k_decay,
        "iota16": np.broadcast_to(np.arange(TOPK), (P, TOPK)),
        "diag8": np.broadcast_to(np.eye(nb).reshape(1, -1), (P, nb * nb)),
        "ret_eye": np.eye(P, nb) * float(rdk) ** -0.5,
    }
    tables = {k: np.ascontiguousarray(v, dtype=f) for k, v in tables.items()}
    return tables, [float(x) for x in np.exp(P * lg)], [float(x) for x in np.exp(lg)]


def kernel(**inputs):
    import numpy as _np
    import concourse.bacc as _bacc
    from concourse import mybir as _mybir
    from concourse.bass_utils import run_bass_kernel_spmd as _run

    nc = _bacc.Bacc("TRN2", target_bir_lowering=False, num_devices=1)
    arrays, args = {}, {}
    for name in _INS:
        x = _np.ascontiguousarray(inputs[name])
        arrays[f"in_{name}_dram"] = x
        args[name] = nc.dram_tensor(f"in_{name}_dram", x.shape, _mybir.dt.from_np(x.dtype), kind="ExternalInput").ap()
    _, seq, d = inputs["x_prompt"].shape
    nb = inputs["x_sample"].shape[0]
    _, _, page, kvl = inputs["cache_ckv"].shape
    rope = inputs["cache_krope"].shape[3]
    _, _, rh, rdk, rdv = inputs["state_ret"].shape
    tables, chunk_decay, gamma = _constants(seq, inputs["page_table"].shape[1] * page, rope, rdk, rh, nb)
    const = {"chunk_decay": chunk_decay, "gamma": gamma}
    for name, x in tables.items():
        arrays[f"const_{name}_dram"] = x
        const[name] = nc.dram_tensor(f"const_{name}_dram", x.shape, _mybir.dt.from_np(x.dtype), kind="ExternalInput").ap()
    outs = {"y_p": (1, seq, d), "y_s": (nb, 1, d), "ckv_p": (1, 1, seq // page, page, kvl),
            "krope_p": (1, 1, seq // page, page, rope), "ret_p": (1, 1, rh, rdk, rdv), "ckv_s": (1, nb, 1, kvl),
            "krope_s": (1, nb, 1, rope), "ret_s": (1, nb, rh, rdk, rdv)}
    out = {n: nc.dram_tensor(f"out_{n}_dram", s, _mybir.dt.from_np(_np.dtype("float32")), kind="ExternalOutput").ap()
           for n, s in outs.items()}
    program(nc, args, out, const)
    r = _run(nc, [arrays], core_ids=[0])
    return tuple(r.results[0][f"out_{n}_dram"] for n in outs)
```

```python
from contextlib import ExitStack

import numpy as np
import concourse.bass as bass
from concourse import mybir

ALU = mybir.AluOpType
ACT = mybir.ActivationFunctionType
F32 = mybir.dt.float32
I32 = mybir.dt.int32
U32 = mybir.dt.uint32
AX = mybir.AxisListType.X
ds = bass.ds

P = 128
EPS = 1e-6
ROPE_BASE = 10000.0
TOPK = 16
NEG = -1e30
GELU_C = float(np.sqrt(2.0 / np.pi))
GELU_A = 0.044715
RSQRT_MAGIC = 1597463007.0


class Signal:

    def __init__(self, sem, per):
        self.sem, self.per = sem, per

    def wait(self, eng, t, k=None):
        value = t * self.per + (self.per if k is None else k)
        if isinstance(value, int) and value <= 0:
            return
        eng.wait_ge(self.sem, value)


class Link:

    def __init__(self, sem, name, per):
        self.sem, self.name, self.per, self.t, self.k, self.dirty = sem, name, per, 0, 0, False

    def begin(self, t):
        self.t, self.k = t, 0

    def __call__(self, eng, ins):
        ins.then_inc(self.sem, 1)
        self.k += 1
        eng.wait_ge(self.sem, self.t * self.per + self.k)

    def mark(self, ins):
        ins.then_inc(self.sem, 1)
        self.k += 1

    def join(self, eng):
        eng.wait_ge(self.sem, self.t * self.per + self.k)

    def end(self):
        assert self.k == self.per, (self.name, "links in a round:", self.k, "declared:", self.per)


class Jobs:

    def __init__(self, filled, drained, names, banks, blocks, rounds=1, before=None):
        self.filled, self.drained, self.banks, self.before, self.blocks = filled, drained, banks, before, blocks
        self.at, self.fills, self.per, self.fills_per = {}, {}, 0, 0
        for name, n in names:
            self.at[name], self.fills[name] = self.per, self.fills_per
            self.per += n
            self.fills_per += 0 if name in blocks else n
        self.total = rounds * self.per
        assert rounds == 1 or self.per % len(banks) == 0

    def bank(self, name, i=0):
        return self.banks[(self.at[name] + i) % len(self.banks)]

    def may_fill(self, pe, t, name, i=0):
        j = self.at[name] + i
        if self.before is not None and j < len(self.banks):
            pe.wait_ge(self.before.drained, self.before.total)
        value = t * self.per + j + 1 - len(self.banks)
        if not isinstance(value, int) or value > 0:
            pe.wait_ge(self.drained, value)

    def wait_filled(self, eng, t, name, i=0):
        assert name not in self.blocks
        eng.wait_ge(self.filled, t * self.fills_per + self.fills[name] + i + 1)

    def wait_drained(self, eng, t, name, i=0):
        value = t * self.per + self.at[name] + i + 1
        if not isinstance(value, int) or value > 0:
            eng.wait_ge(self.drained, value)


def program(nc, a, out, const):
    _, SEQ, D = a["x_prompt"].shape
    NB = a["x_sample"].shape[0]
    _, NPHYS, PAGE, KVL = a["cache_ckv"].shape
    ROPE = a["cache_krope"].shape[3]
    _, _, RH, RDK, RDV = a["state_ret"].shape
    NPAGES = a["page_table"].shape[1]
    QL = a["q_norm_g"].shape[1]
    NH = a["w_uk"].shape[2]
    NOPE = a["w_uk"].shape[3]
    VH = a["w_uv"].shape[3]
    _, _, PH, NK, PD = a["peer_sub_keys"].shape
    assert PAGE == P and NK == P and PD == P and RDK == P and D == 1024 and NB == 8
    HD = NOPE + ROPE
    T = SEQ // P
    KC = D // P
    QC = QL // P
    SCALE = float(HD) ** -0.5
    O_CKV, O_KR = QL, QL + KVL
    O_RQ = O_KR + ROPE
    O_RV = O_RQ + 2 * RH * RDK
    O_RG = O_RV + RH * RDV
    O_GA = O_RG + RH * RDV
    RING = 8

    w_in, w_uq, w_oa, w_ob, w_out, w_q = (a[n][0] for n in ("w_in", "w_uq", "w_oa", "w_ob", "w_out", "peer_w_q"))
    BW = 256
    stream = [("linA", w_in, c, min(BW, O_RG - c)) for c in range(0, O_RG, BW)]
    NA = len(stream)
    stream += [("uq", w_uq, c, BW) for c in range(0, NH * HD, BW)]
    stream += [("rg", w_in, O_RG + c, BW) for c in range(0, D, BW)]
    stream += [("ob", w_ob, c, BW) for c in range(0, D, BW)]
    stream += [("oa", w_oa, c, 512) for c in range(0, D, 512)]
    stream += [("gate", w_in, O_GA + c, BW) for c in range(0, 2 * D, BW)]
    stream += [("out", w_out, c, BW) for c in range(0, D, BW)]
    stream += [("wq", w_q, c, BW) for c in range(0, 2 * PH * PD, BW)]
    NBLK = len(stream)
    WSLOTS = 2
    assert NBLK % WSLOTS == 0
    first = {}
    for n, (name, _, _, _) in enumerate(stream):
        first.setdefault(name, n)

    with ExitStack() as ctx:
        def sb(name, words, dt=F32):
            return ctx.enter_context(nc.sbuf_tensor(name, [P, words], dt))

        def sem(name):
            return ctx.enter_context(nc.semaphore(name))

        def signal(name, per=1):
            return Signal(sem(name), per)

        def grid(ap, n):
            return ap.rearrange("p (a b) -> p a b", a=n)

        ident = sb("ident", P)
        ffn_gain = sb("ffn_gain", D)
        final_gain = sb("final_gain", D)
        kv_gain = sb("kv_gain", KVL)
        attn_gain_t = sb("attn_gain_t", KC)
        q_gain_t = sb("q_gain_t", QC)
        ret_gain_t = sb("ret_gain_t", KC)
        decay_t = sb("decay_t", RH * P)
        q_decay = sb("q_decay", RH * P)
        k_decay = sb("k_decay", RH)
        iota16 = sb("iota16", TOPK)
        diag8 = sb("diag8", NB * NB)
        ret_eye = sb("ret_eye", NB)
        uk = sb("uk", 2 * NH * NOPE)
        uv = sb("uv", 2 * NH * VH)
        keys_t = sb("keys_t", 2 * PH * P)
        pages_reg = sb("pages_reg", NB * NPAGES, I32)
        KV = sb("KV", max(NH * SEQ, NPAGES * KVL) + max(T * NH * VH, NPAGES * ROPE + 3072))
        VAT = max(NH * SEQ, NPAGES * KVL)
        key_t = KV[:, 0:NH * SEQ].rearrange("p (h s) -> p h s", h=NH)
        value = KV[:, VAT:VAT + T * NH * VH].rearrange("p (t c) -> p t c", t=T)
        state = sb("state", RH * RDV)
        rows = sb("rows", RING * D)
        wbuf = sb("wbuf", WSLOTS * KC * BW)
        px = sb("px", D)
        py = [sb("py0", D), sb("py1", D)]
        pe_id = sb("pe_id", P, U32)
        pe_id_s = [sb(f"pe_id_s{i}", TOPK, U32) for i in range(2)]
        pg = sb("pg", P)
        dots = sb("dots", TOPK)
        ga_, gb_, gcoef = sb("ga_", TOPK), sb("gb_", TOPK), sb("gcoef", TOPK)
        fin = sb("fin", 8)
        xin = sb("xin", D)
        xt = sb("xt", D)
        z = sb("z", O_RG)
        WK = sb("WK", max(4 * D, NPAGES * P) + 8)
        sc = [WK[:, 0:D], WK[:, 3 * D:4 * D]]
        pt = WK[:, D:2 * D]
        maskb = WK[:, 2 * D:3 * D]
        xn2 = maskb
        oa = WK[:, 3 * D:4 * D]
        rqk = WK[:, 3 * D:4 * D]
        rqt, rqd, rkt, kd = (WK[:, i * 512:(i + 1) * 512] for i in range(4))
        at = WK[:, 3 * D:3 * D + 512]
        t2 = sb("t2", D)
        oret = sb("oret", D)
        qb = sb("qb", NH * HD)
        knat = sb("knat", NH * HD)
        qt = sb("qt", NH * P)
        ropeb = sb("ropeb", 3 * (RDK // 2) + 3 * (ROPE // 2))
        rt = sb("rt", 2 * NH * ROPE)
        stat = sb("stat", 16)
        nr = sb("nr", 48)
        mx, nmx, sums = sb("mx", NH), sb("nmx", NH), sb("sums", NH)
        rstat = sb("rstat", 4 * RH)
        ssq = sb("ssq", 2 * PH)
        rstd_q = sb("rstd_q", 2 * PH)
        sv = sb("sv", 2 * PH * TOPK)
        si = sb("si", 2 * PH * TOPK, U32)
        sif = sb("sif", 2 * PH * TOPK)
        ts_ = sb("ts_", P)
        tp = sb("tp", P, U32)
        tq = sb("tq", P, U32)
        tf = sb("tf", P)
        i0, i1 = sb("i0", P), sb("i1", P)
        eid = sb("eid", P, U32)
        gw = sb("gw", P)
        gs = sb("gs", 2 * PH)
        qs = sb("qs", 3 * NH + 3)
        cuts = [0]

        def cut(words):
            cuts.append(cuts[-1] + words)
            assert cuts[-1] <= NH * P
            return qt[:, cuts[-2]:cuts[-1]]

        qabs = cut(3 * NH * NB)
        nkr = cut(NB)
        qmb = cut(RH * NB)
        ptb = cut(NPAGES * NH)
        psl = cut(2 * NB)
        ota = cut(2 * NH * NB)
        o_lat = cut(KVL)
        kmb = qb[:, 0:RH * RDK]
        p_owner = decay_t[0:NB, 0:P]
        p_rank = decay_t[0:TOPK, P:2 * P]
        p_sel = decay_t[:, 2 * P:2 * P + NB + TOPK]
        p_tmp = decay_t[:, 3 * P:4 * P]
        p_idf, p_wt, p_dots, p_ga, p_gb, p_coef = (q_decay[:, i * PH:(i + 1) * PH] for i in range(6))
        p_selc = q_decay[:, P:P + PH * NB]
        p_id = eid[:, 0:PH]
        p_x = t2
        p_u = [rows[:, i * D:(i + 1) * D] for i in range(4)] + [WK[:, i * D:(i + 1) * D] for i in range(4)]
        p_v = [KV[:, i * D:(i + 1) * D] for i in range(7)] + [xt[:, :]]
        PS = ctx.enter_context(nc.psum_tensor("PS", [P, 8 * 512], F32))
        bank = [PS[:, i * 512:(i + 1) * 512] for i in range(8)]

        const_in = sem("const_in")
        setup_in = sem("setup_in")
        zeroed = sem("zeroed")
        x_in = signal("x_in", 48)
        w_in_s = [signal(f"w_arrived{i}", 16 * (NBLK // WSLOTS)) for i in range(WSLOTS)]
        w_used = signal("w_used", NBLK)
        a_names = [("xT", 2), ("linA", NA), ("qlT", 1), ("ckT", 1), ("rqT", 1), ("rkT", 1), ("knat", 1), ("value", 1),
                   ("uq", 3), ("reto", 2), ("keyT", 2), ("qT", 2), ("probT", NH * (-(-T // 4))), ("rg", 4), ("bT", 2),
                   ("ob", 4), ("ovT", 1), ("oa", 2), ("gate", 8), ("mT", 2), ("x2T", 2), ("wq", 2 * PH * PD // BW),
                   ("pqT", 4)]
        blocks = set(first)
        A = Jobs(sem("act_filled"), sem("act_drained"), a_names,
                 bank[0:3 if sum(n for _, n in a_names) % 3 == 0 else 1], blocks, T)
        DJ = Jobs(sem("dve_filled"), sem("dve_drained"),
                 [("retA", 1), ("stateU", 1), ("score", NH), ("out", 2), ("pscore", 2)], [PS[:, 4 * 512:6 * 512]], blocks, T)
        KJ = Jobs(sem("keys_filled"), sem("keys_drained"), [("keys", 4)], bank[0:4], blocks)
        s_names = [("xT", 2), ("linA", NA), ("qlT", 1), ("ckT", 1), ("rqT", 1), ("uq", 3), ("qnT", 1), ("qrT", 1),
                   ("ukT", 4), ("qabs", 1), ("rg", 4), ("bT", 2), ("ob", 4), ("ovT", 1), ("oa", 2), ("gate", 8),
                   ("mT", 2), ("x2T", 2), ("wq", 2 * PH * PD // BW), ("pqT", 4)]
        AS = Jobs(sem("s_act_filled"), sem("s_act_drained"), s_names, bank[0:2], blocks, 1, A)
        DS = Jobs(sem("s_dve_filled"), sem("s_dve_drained"), [("out", 2), ("pscore", 2)], [PS[:, 4 * 512:6 * 512]],
                  blocks, 1, DJ)
        x_normed = signal("x_normed")
        lat_normed = signal("lat_normed")
        krope_ready = signal("krope_ready")
        ret_roped = signal("ret_roped")
        k_decayed = signal("k_decayed")
        q_roped = signal("q_roped")
        q_decayed = signal("q_decayed")
        keys_read = sem("keys_read")
        max_ready = signal("max_ready", NH)
        probs_ready = signal("probs_ready", NH)
        pv_done = signal("pv_done")
        heads_normed = signal("heads_normed")
        ret_negmean = signal("ret_negmean")
        ret_squares = signal("ret_squares")
        ret_rstd = signal("ret_rstd")
        ret_normed = signal("ret_normed", RH)
        ret_gated = signal("ret_gated")
        merged = signal("merged")
        x2_normed = signal("x2_normed")
        q_rstd_in = signal("q_rstd_in")
        top_shifted = signal("top_shifted")
        top_exp = signal("top_exp")
        chosen = signal("chosen")
        committed = signal("committed")
        ckv_stored = sem("ckv_stored")
        fd = Link(sem("front_steps"), "front", FRONT_LINKS)
        pdl = Link(sem("expert_steps"), "experts", EXPERT_LINKS)
        gate_pool, gate_dve, gate_pe, gate_sp = (sem(f"{e}_passed") for e in ("pool", "dve", "pe", "sp"))
        row_in = [sem(f"row_arrived{i}") for i in range(RING)]
        u_used = signal("u_used", P)
        v_pe_used = signal("v_pe_used", P // SHARE)
        v_dve_used = signal("v_dve_used", P - P // SHARE)

        def u_row_used(h, k):
            return u_used, h * TOPK + k + 1

        def v_row_used(h, k):
            if k % SHARE == SHARE - 1:
                return v_pe_used, h * (TOPK // SHARE) + k // SHARE + 1
            return v_dve_used, h * (TOPK - TOPK // SHARE) + k + 1 - k // SHARE
        staged = sem("ids_staged")
        gelu_in = signal("gelu_in", PH)
        coefs_ready = signal("coefs_ready", PH)
        diag_ready = signal("diag_ready", P // SHARE)
        gelu_tanh = signal("gelu_tanh", PH)
        y_ready = signal("y_ready")
        y_stored = sem("y_stored")
        state_out = sem("state_out")
        table_in = sem("table_in")
        s_state_in = signal("s_state_in", 16)
        s_state_new = signal("s_state_new")
        s_state_stored = signal("s_state_stored", 16)
        s_masked = signal("s_masked", 2)
        s_outer = signal("s_outer")
        s_oret = signal("s_oret")
        s_oret_added = signal("s_oret_added", 2)
        s_zero = sem("s_zero")
        s_ret_sum = sem("s_ret_sum")
        s_staged = signal("s_staged", 4)
        NCH = NPAGES // 4
        s_pages = [signal(f"s_pages{c}", 8 * 16) for c in range(NCH)]
        s_pv = signal("s_pv", NCH + 1)
        s_kt_filled = signal("s_kt_filled", 3 * NCH)
        s_kt_drained = signal("s_kt_drained", 3 * NCH)
        s_sc_filled = signal("s_sc_filled", NCH + 1)
        s_sc_drained = signal("s_sc_drained", NCH + 1)
        s_max = signal("s_max", NCH + 3)
        s_exp = signal("s_exp")
        s_prob = signal("s_prob", 2)
        s_pt_filled = signal("s_pt_filled", 2)
        s_pt_drained = signal("s_pt_drained", 2)
        s_ot_filled = signal("s_ot_filled")
        s_ot_drained = signal("s_ot_drained", 2)
        s_ov_filled = sem("s_ov_filled")
        p_built = sem("p_built")
        p_spread = sem("p_spread")
        p_ids = sem("p_ids")
        p_rows_out = sem("p_rows_out")
        p_u_in = [sem(f"p_u_arrived{h}") for h in range(PH)]
        p_v_in = sem("p_v_arrived")
        p_gelu_in = sem("p_gelu_in")
        p_tanh = sem("p_tanh")
        p_coefs = sem("p_coefs")
        p_summed = sem("p_summed")

        block = ctx.enter_context(nc.Block())

        def sp_front(sp, t, sample=False):
            committed.wait(sp, t, 0)
            if sample:
                sp.wait_ge(s_zero, 1)
                sp.dma_start(xin[0:NB, :], a["x_sample"].rearrange("b s d -> (b s) d")).then_inc(x_in.sem, 16)
            else:
                sp.dma_start(xin[:, :], a["x_prompt"][0][ds(t * P, P), :]).then_inc(x_in.sem, 16)
            sp.dma_start(ropeb[:, :], const["rope"][ds(t * P, P), :]).then_inc(x_in.sem, 16)
            if not sample:
                sp.dma_start(maskb[:, 0:SEQ], const["mask"][:, ds((T - 1 - t) * P, SEQ)]).then_inc(x_in.sem, 16)

            def blocks(name):
                for n, (nm, w, c, wd) in enumerate(stream):
                    if nm != name:
                        continue
                    w_used.wait(sp, t, n + 1 - WSLOTS)
                    k = w.shape[0] // P
                    dst = wbuf[:, (n % WSLOTS) * KC * BW:(n % WSLOTS) * KC * BW + k * wd]
                    sp.dma_start(dst.rearrange("p (k c) -> p k c", k=k),
                                 w[:, c:c + wd].rearrange("(k p) c -> p k c", p=P)).then_inc(w_in_s[n % WSLOTS].sem, 16)

            blocks("linA")
            blocks("uq")
            krope_ready.wait(sp, t)
            if sample:
                sp.dma_start(out["ckv_s"].rearrange("l b s c -> (l b s) c"), z[0:NB, O_CKV:O_KR]).then_inc(ckv_stored, 16)
                sp.dma_start(out["krope_s"].rearrange("l b s c -> (l b s) c"), knat[0:NB, NOPE:HD]).then_inc(ckv_stored, 16)
            else:
                sp.dma_start(out["ckv_p"][0, 0].rearrange("n p c -> (n p) c")[ds(t * P, P), :],
                             z[:, O_CKV:O_KR]).then_inc(ckv_stored, 16)
                sp.dma_start(out["krope_p"][0, 0].rearrange("n p c -> (n p) c")[ds(t * P, P), :],
                             knat[:, NOPE:HD]).then_inc(ckv_stored, 16)
            if sample:
                sp_sample(sp)
            for name in ("rg", "ob", "oa", "gate", "out", "wq"):
                blocks(name)

        def sp_store_y(sp, t, n=P):
            y_ready.wait(sp, t)
            dst = (out["y_p"][0][ds(t * P, P), :] if n == P else out["y_s"].rearrange("b s d -> (b s) d"))
            sp.dma_start(dst, py[1][0:n, :]).then_inc(y_stored, 16)

        def s_state_buf(b):
            return KV[:, VAT + NPAGES * ROPE:VAT + NPAGES * ROPE + RH * RDV]

        def sp_sample(sp):
            pv_done.wait(sp, T - 1)

            def load_state(b):
                sp.dma_start(s_state_buf(b).rearrange("p (h e) -> p h e", h=RH),
                             a["state_ret"][0][ds(b, 1)].rearrange("o h d e -> d (o h) e")).then_inc(s_state_in.sem, 16)

            def load_pages(b, c):
                numbers = [sp.value_load(pages_reg[0:1, ds(b * NPAGES + 4 * c + k, 1)], min_val=0, max_val=NPHYS - 1)
                           for k in range(4)]
                for k, page in enumerate(numbers):
                    p = 4 * c + k
                    sp.dma_start(KV[:, p * KVL:(p + 1) * KVL],
                                 a["cache_ckv"][0][ds(page, 1)].rearrange("o p c -> (o p) c")).then_inc(s_pages[c].sem, 16)
                    sp.dma_start(KV[:, VAT + p * ROPE:VAT + (p + 1) * ROPE],
                                 a["cache_krope"][0][ds(page, 1)].rearrange("o p c -> (o p) c")).then_inc(s_pages[c].sem, 16)

            for b in range(NB):
                s_oret.wait(sp, b - 1)
                s_state_stored.wait(sp, b - 1)
                load_state(b)
                for c in range(NCH):
                    if c * NB // NCH == b:
                        load_pages(0, c)
                s_state_new.wait(sp, b)
                sp.dma_start(out["ret_s"][0][b:b + 1].rearrange("o h d e -> d (o h) e"),
                             s_state_buf(b).rearrange("p (h e) -> p h e", h=RH)).then_inc(s_state_stored.sem, 16)
            with sp.Fori(1, NB) as b:
                for c in range(NCH):
                    s_pv.wait(sp, b - 1, c + 1)
                    sp.sem_inc(gate_sp, 1)
                    load_pages(b, c)

        @block.sync
        def _(sp):
            n = 0
            for dst, src in ((ident[:, :], const["ident"]), (decay_t[:, :], const["decay"]), (q_decay[:, :], const["q_decay"]),
                             (k_decay[:, :], const["k_decay"]), (iota16[:, :], const["iota16"]), (diag8[:, :], const["diag8"]),
                             (ret_eye[:, :], const["ret_eye"]),
                             (ffn_gain[:, :], a["ffn_norm_g"].broadcast_to([P, D])),
                             (final_gain[:, :], a["final_norm_g"].rearrange("(a d) -> a d", a=1).broadcast_to([P, D])),
                             (kv_gain[:, :], a["kv_norm_g"].broadcast_to([P, KVL])),
                             (uk[:, :].rearrange("p (k c) -> p k c", k=2), a["w_uk"][0].rearrange("(k p) h n -> p k (h n)", p=P)),
                             (uv[:, :].rearrange("p (k c) -> p k c", k=2), a["w_uv"][0].rearrange("(k p) h n -> p k (h n)", p=P)),
                             ):
                sp.dma_start(dst, src).then_inc(const_in, 16)
                n += 16
            with nc.allow_non_contiguous_dma("gains are read once, one value per partition"):
                for dst, src in ((attn_gain_t, a["attn_norm_g"]), (q_gain_t, a["q_norm_g"]), (ret_gain_t, a["ret_norm_g"])):
                    sp.dma_start(dst[:, :], src[0].rearrange("(k p) -> p k", p=P)).then_inc(const_in, 16)
                    n += 16
            assert n == CONST_LOADS * 16
            sp.dma_start(rows[:, 0:2 * PH * PD].rearrange("p (g d) -> p g d", g=2 * PH),
                         a["peer_sub_keys"][0].rearrange("s h k d -> k (s h) d")).then_inc(setup_in, 16)
            sp.dma_start(pages_reg[0:1, :], a["page_table"].rearrange("(o b) n -> o (b n)", o=1)).then_inc(table_in, 16)
            sp.wait_ge(table_in, 16)
            sp_front(sp, 0)
            sp_front(sp, 1)
            sp_store_y(sp, 0)
            with sp.Fori(1, T - 1) as t:
                sp_front(sp, t + 1)
                sp_store_y(sp, t)
            sp_front(sp, T, sample=True)
            DJ.wait_drained(sp, T - 1, "stateU")
            sp.dma_start(out["ret_p"][0, 0].rearrange("h d e -> d h e"),
                         state[:, :].rearrange("p (h e) -> p h e", h=RH)).then_inc(state_out, 16)
            sp_store_y(sp, T - 1)
            sp_store_y(sp, T, NB)
            sp.wait_ge(state_out, 16)
            sp.wait_ge(y_stored, 16 * (T + 1))
            sp.wait_ge(ckv_stored, 32 * (T + 1))
            sp.wait_ge(s_state_stored.sem, 16 * NB)

        def pool_wait(pool, sig, t, count):
            value_ = t * sig.per + count
            if not isinstance(value_, int) or value_ > 0:
                pool.wait_ge(sig.sem, value_)
                pool.sem_inc(gate_pool, 1)

        def pool_gathers(pool, t, h, s):
            for own, other, other_h, table in ((u_row_used, v_row_used, h - 1, a["peer_u"][0]),
                                               (v_row_used, u_row_used, h, a["peer_v"][0])):
                for k in range(TOPK):
                    slot = k % RING
                    sig, count = own(h, k - RING) if k >= RING else other(other_h, k + TOPK - RING)
                    pool_wait(pool, sig, t, count)
                    pool.indirect_dma_start(rows[:, slot * D:(slot + 1) * D], None, table,
                                            bass.IndirectOffsetOnAxis(ap=pe_id_s[s][:, k:k + 1], axis=0)
                                            ).then_inc(row_in[slot], 16)

        def pool_head(pool, t, h, s):
            for sig in (v_pe_used, v_dve_used):
                pool_wait(pool, sig, t, (h - 1) * (sig.per // PH))
            nc.gpsimd.tensor_copy(pe_id_s[s][:, :], pe_id[:, ds(h * TOPK, TOPK)]).then_inc(staged, 1)
            pool.wait_ge(staged, t * PH + h + 1)
            pool.sem_inc(gate_pool, 1)
            pool_gathers(pool, t, h, s)

        @block.gpsimd
        def _(pool):
            nc.gpsimd.memset(KV[:, :], 0.0).then_inc(zeroed, 1)
            nc.gpsimd.memset(state[:, :], 0.0).then_inc(zeroed, 1)

            def tile(t, start=0):
                committed.wait(pool, t)
                pool.sem_inc(gate_pool, 1)
                if start:
                    for h in range(start):
                        pool_head(pool, t, h, h % 2)
                with pool.Fori(start // 2, PH // 2) as i:
                    pool_head(pool, t, 2 * i, 0)
                    pool_head(pool, t, 2 * i + 1, 1)

            pool.wait_ge(keys_read, 1)
            tile(0, start=2)
            with pool.Fori(1, T) as t:
                tile(t)
            pool.wait_ge(p_ids, 1)
            for table, places in ((a["peer_u"][0], p_u), (a["peer_v"][0], p_v)):
                for h in range(PH):
                    pool.indirect_dma_start(places[h], None, table, bass.IndirectOffsetOnAxis(ap=p_id[:, h:h + 1], axis=0)
                                            ).then_inc(p_u_in[h] if places is p_u else p_v_in, 16)

        checkpoints = []

        def beside(front, experts):
            checkpoints.append([(at_, next(experts, None)) for at_ in front] + list(experts))

        def diag(k):
            return py[1][:, (k // SHARE) * P:(k // SHARE + 1) * P]

        def transposes(J, t, pe, name, i, chunks, n=P, m=P):
            J.may_fill(pe, t, name, i)
            b = J.bank(name, i)
            for k, src in enumerate(chunks):
                last = nc.tensor.transpose(b[0:m, k * n:(k + 1) * n], src, ident[0:n, 0:n])
            last.then_inc(J.filled, 1)

        NPT = -(-T // 4)

        def key_tiles(t):
            return -(-2 // NPT) if isinstance(t, int) and t < 2 else min(4, T)

        def pe_block(pe, J, t, name, i, lhs, bnk=None, inc=True):
            n = first[name] + i
            _, w, _, wd = stream[n]
            k = w.shape[0] // P
            w_in_s[n % WSLOTS].wait(pe, t, 16 * (n // WSLOTS + 1))
            if bnk is None:
                J.may_fill(pe, t, name, i)
                bnk = J.bank(name, i)[:, 0:wd]
            base = (n % WSLOTS) * KC * BW
            for j in range(k):
                last = nc.tensor.matmul(bnk, lhs[:, j * P:(j + 1) * P], wbuf[:, base + j * wd:base + (j + 1) * wd],
                                        start=(j == 0), stop=(j == k - 1))
            last.then_inc(w_used.sem, 1)

        def pe_front(pe, t, sample=False):
            J, DD = (AS, DS) if sample else (A, DJ)
            tj = 0 if sample else t
            x_normed.wait(pe, t)
            for i in range(2):
                transposes(J, tj, pe, "xT", i, [sc[0][:, (4 * i + k) * P:(4 * i + k + 1) * P] for k in range(4)])
            yield "xT"
            J.wait_drained(pe, tj, "xT", 1)
            for i in range(NA):
                pe_block(pe, J, tj, "linA", i, xt) if not sample else pe_block_s(pe, J, t, "linA", i, xt)
                yield "lin"
            lat_normed.wait(pe, t)
            transposes(J, tj, pe, "qlT", 0, [z[:, k * P:(k + 1) * P] for k in range(QC)])
            transposes(J, tj, pe, "ckT", 0, [z[:, O_CKV + k * P:O_CKV + (k + 1) * P] for k in range(2)])
            ret_roped.wait(pe, t)
            transposes(J, tj, pe, "rqT", 0, [rqk[:, h * P:(h + 1) * P] for h in range(RH)])
            if not sample:
                transposes(J, tj, pe, "rkT", 0, [rqk[:, (RH + h) * P:(RH + h + 1) * P] for h in range(RH)])
                J.wait_drained(pe, tj, "ckT")
                for name, w in (("knat", uk), ("value", uv)):
                    J.may_fill(pe, tj, name)
                    for c in range(2):
                        last = nc.tensor.matmul(J.bank(name), t2[:, (3 + c) * P:(4 + c) * P], w[:, c * 512:(c + 1) * 512],
                                                start=(c == 0), stop=(c == 1))
                    last.then_inc(J.filled, 1)
            yield "lat"
            J.wait_drained(pe, tj, "qlT")
            for i in range(3):
                pe_block(pe, J, tj, "uq", i, t2) if not sample else pe_block_s(pe, J, t, "uq", i, t2)
                yield "uq"
            if sample:
                pe_sample(pe)
                for name in ("reto", "squares", "normed"):
                    yield name
                pe_sample_attention(pe)
                yield "keys"
            else:
                J.wait_drained(pe, tj, "rkT")
                DD.may_fill(pe, tj, "retA")
                rb = DD.bank("retA")
                for h in range(RH):
                    last = nc.tensor.matmul(rb[:, h * P:(h + 1) * P], rkt[:, h * P:(h + 1) * P], rqt[:, h * P:(h + 1) * P],
                                            start=True, stop=True)
                last.then_inc(DD.filled, 1)
                DD.wait_drained(pe, tj, "retA")
                q_decayed.wait(pe, t)
                DD.wait_drained(pe, t - 1, "stateU")
                if isinstance(t, int) and t == 0:
                    pe.wait_ge(zeroed, 2)
                for i in range(2):
                    J.may_fill(pe, tj, "reto", i)
                    for h in (2 * i, 2 * i + 1):
                        o = J.bank("reto", i)[:, (h % 2) * RDV:(h % 2 + 1) * RDV]
                        nc.tensor.matmul(o, at[:, h * P:(h + 1) * P], z[:, O_RV + h * RDV:O_RV + (h + 1) * RDV],
                                         start=True, stop=False)
                        last = nc.tensor.matmul(o, rqd[:, h * P:(h + 1) * P], state[:, h * RDV:(h + 1) * RDV],
                                                start=False, stop=True)
                    last.then_inc(J.filled, 1)
                k_decayed.wait(pe, t)
                DD.may_fill(pe, tj, "stateU")
                for h in range(RH):
                    last = nc.tensor.matmul(DD.bank("stateU")[:, h * RDV:(h + 1) * RDV], kd[:, h * P:(h + 1) * P],
                                            z[:, O_RV + h * RDV:O_RV + (h + 1) * RDV], start=True, stop=True)
                last.then_inc(DD.filled, 1)
                for name in ("reto", "squares", "normed"):
                    yield name
                krope_ready.wait(pe, t)
                J.wait_drained(pe, tj, "knat")
                for i in range(2):
                    transposes(J, tj, pe, "keyT", i, [knat[:, (4 * i + k) * HD:(4 * i + k + 1) * HD] for k in range(4)], m=HD)
                q_roped.wait(pe, t)
                for i in range(2):
                    transposes(J, tj, pe, "qT", i, [qb[:, (4 * i + k) * HD:(4 * i + k + 1) * HD] for k in range(4)], m=HD)
                yield "keys"
                J.wait_drained(pe, tj, "qT", 1)

                def scores(h):
                    DD.may_fill(pe, tj, "score", h)
                    for i in range(0, NPT * KT * P, 512):
                        w = min(512, NPT * KT * P - i)
                        last = nc.tensor.matmul(DD.bank("score", h)[:, i:i + w], qt[0:HD, h * P:(h + 1) * P],
                                                key_t[0:HD, h, i:i + w], start=True, stop=True)
                    last.then_inc(DD.filled, 1)

                KT = key_tiles(t)
                scores(0)
                for h in range(NH):
                    if h + 1 < NH:
                        scores(h + 1)
                    probs_ready.wait(pe, t, h + 1)
                    for i in range(NPT):
                        transposes(J, tj, pe, "probT", NPT * h + i,
                                   [sc[h % 2][:, (KT * i + k) * P:(KT * i + k + 1) * P] for k in range(KT)])
                    if h == 0:
                        heads_normed.wait(pe, t - 1)
                    for k in range(NPT * KT):
                        if k % KT == 0:
                            J.wait_drained(pe, tj, "probT", NPT * h + k // KT)
                        last = nc.tensor.matmul(bank[6][:, h * VH:(h + 1) * VH], pt[:, k * P:(k + 1) * P],
                                                value[:, k, h * VH:(h + 1) * VH], start=(k == 0), stop=(k == NPT * KT - 1))
                    if h == NH - 1:
                        last.then_inc(pv_done.sem, 1)
                    yield "head"
            blk = (lambda name, i, lhs, b=None: pe_block_s(pe, J, t, name, i, lhs, b)) if sample else \
                (lambda name, i, lhs, b=None: pe_block(pe, J, tj, name, i, lhs, b))
            for i in range(4):
                blk("rg", i, xt)
                yield "rg"
            ret_gated.wait(pe, t)
            for i in range(2):
                transposes(J, tj, pe, "bT", i, [oret[:, (4 * i + k) * P:(4 * i + k + 1) * P] for k in range(4)])
            J.wait_drained(pe, tj, "bT", 1)
            for i in range(4):
                blk("ob", i, t2)
                yield "ob"
            heads_normed.wait(pe, t)
            transposes(J, tj, pe, "ovT", 0, [qb[:, k * P:(k + 1) * P] for k in range(4)])
            J.wait_drained(pe, tj, "ovT")
            for i in range(2):
                blk("oa", i, t2)
                yield "oa"
            for i in range(8):
                blk("gate", i, xt)
                yield "gate"
            merged.wait(pe, t)
            for i in range(2):
                transposes(J, tj, pe, "mT", i, [oa[:, (4 * i + k) * P:(4 * i + k + 1) * P] for k in range(4)])
            yield "merge"
            J.wait_drained(pe, tj, "mT", 1)
            for i in range(4):
                if i % 2 == 0:
                    DD.may_fill(pe, tj, "out", i // 2)
                blk("out", i, t2, DD.bank("out")[:, (i % 2) * 256:(i % 2) * 256 + 256])
            yield "out"
            x2_normed.wait(pe, t)
            for i in range(2):
                transposes(J, tj, pe, "x2T", i, [xn2[:, (4 * i + k) * P:(4 * i + k + 1) * P] for k in range(4)])
            yield "x2"
            J.wait_drained(pe, tj, "x2T", 1)
            for i in range(2 * PH * PD // BW):
                blk("wq", i, xt)
                yield "wq"
            J.wait_drained(pe, tj, "wq", 2 * PH * PD // BW - 1)
            for i in range(4):
                transposes(J, tj, pe, "pqT", i, [z[:, (4 * i + k) * P:(4 * i + k + 1) * P] for k in range(4)])
            for i in range(2):
                DD.may_fill(pe, tj, "pscore", i)
                for h in range(PH):
                    if h % 2 == 0:
                        J.wait_drained(pe, tj, "pqT", h // 2)
                    q, g = 2 * h + i, i * PH + h
                    last = nc.tensor.matmul(DD.bank("pscore", i)[:, h * P:(h + 1) * P], WK[:, q * P:(q + 1) * P],
                                            keys_t[:, g * P:(g + 1) * P], start=True, stop=True)
                last.then_inc(DD.filled, 1)
                if i == 0:
                    yield "pqT"
            for _ in range(TOPK_YIELDS):
                yield "top"
            yield "end"

        def pe_block_s(pe, J, t, name, i, lhs, bnk=None):
            if bnk is None:
                J.may_fill(pe, 0, name, i)
                bnk = J.bank(name, i)[:, 0:stream[first[name] + i][3]]
            pe_block(pe, J, t, name, i, lhs, bnk)

        def pe_sample(pe):
            q_roped.wait(pe, T)
            AS.may_fill(pe, 0, "qnT")
            for h in range(NH):
                last = nc.tensor.transpose(AS.bank("qnT")[0:NOPE, h * NB:(h + 1) * NB], qb[0:NB, h * HD:h * HD + NOPE],
                                           ident[0:NB, 0:NB])
            last.then_inc(AS.filled, 1)
            AS.may_fill(pe, 0, "qrT")
            for h in range(NH):
                nc.tensor.transpose(AS.bank("qrT")[0:ROPE, h * NB:(h + 1) * NB], qb[0:NB, h * HD + NOPE:(h + 1) * HD],
                                    ident[0:NB, 0:NB])
            krope_ready.wait(pe, T)
            nc.tensor.transpose(AS.bank("qrT")[0:ROPE, NH * NB:(NH + 1) * NB], knat[0:NB, NOPE:HD],
                                ident[0:NB, 0:NB]).then_inc(AS.filled, 1)
            pe.wait_ge(DJ.drained, DJ.total)
            heads_normed.wait(pe, T - 1)

            def ret(b):
                s_masked.wait(pe, b)
                s_state_new.wait(pe, b, 0)
                for h in range(RH):
                    last = nc.tensor.matmul(PS[:, 4 * 512 + h * RDV:4 * 512 + (h + 1) * RDV], kmb[0:NB, h * P:(h + 1) * P],
                                            z[0:NB, O_RV + h * RDV:O_RV + (h + 1) * RDV], start=True, stop=True)
                last.then_inc(s_outer.sem, 1)
                s_state_new.wait(pe, b)
                s_oret_added.wait(pe, b, 0)
                for h in range(RH):
                    o = bank[6 if h < 2 else 2][0:NB, (h % 2) * RDV:(h % 2 + 1) * RDV]
                    last = nc.tensor.matmul(o, qmb[:, h * NB:(h + 1) * NB],
                                            s_state_buf(b)[:, h * RDV:(h + 1) * RDV], start=True, stop=True)
                last.then_inc(s_oret.sem, 1)

            ret(0)
            with pe.Fori(1, NB) as b:
                ret(b)

            for i in range(4):
                AS.may_fill(pe, 0, "ukT", i)
                for k in range(4):
                    g = 4 * i + k
                    last = nc.tensor.transpose(AS.bank("ukT", i)[0:NOPE, k * P:(k + 1) * P],
                                               uk[:, (g % 2) * 512 + (g // 2) * NOPE:(g % 2) * 512 + (g // 2 + 1) * NOPE], ident[:, :])
                last.then_inc(AS.filled, 1)
            AS.wait_drained(pe, 0, "ukT", 3)
            AS.may_fill(pe, 0, "qabs")
            for g in range(2 * NH):
                last = nc.tensor.matmul(AS.bank("qabs")[:, ((g % 2) * NH + g // 2) * NB:((g % 2) * NH + g // 2 + 1) * NB],
                                        ukt[0:NOPE, g * P:(g + 1) * P],
                                        psq[0:NOPE, (g // 2) * NB:(g // 2 + 1) * NB], start=True, stop=True)
            last.then_inc(AS.filled, 1)

            AS.wait_drained(pe, 0, "qabs")
            s_oret_added.wait(pe, NB - 1)

        def pe_sample_attention(pe):
            ktb = [KV[:, VAT + NPAGES * ROPE + i * 1536:VAT + NPAGES * ROPE + (i + 1) * 1536] for i in range(2)]

            def attend(b):
                s_staged.wait(pe, b)

                def turn(c):
                    s_pages[c].wait(pe, b)
                    for part in range(3):
                        s_kt_drained.wait(pe, b, 3 * c + part - 2)
                        w = P if part < 2 else ROPE
                        for k in range(4):
                            pg_ = 4 * c + k
                            src = KV[:, pg_ * KVL + part * P:pg_ * KVL + (part + 1) * P] if part < 2 else \
                                KV[:, VAT + pg_ * ROPE:VAT + (pg_ + 1) * ROPE]
                            last = nc.tensor.transpose(bank[part][0:w, k * P:(k + 1) * P], src, ident[:, :])
                        last.then_inc(s_kt_filled.sem, 1)

                def score(c):
                    s_kt_drained.wait(pe, b, 3 * c + 3)
                    s_sc_drained.wait(pe, b, c - 1)
                    if c == 0:
                        s_ot_drained.wait(pe, b, 0)
                    for part in range(3):
                        w = P if part < 2 else ROPE
                        last = nc.tensor.matmul(bank[4 + c % 2][0:NH, :], qs[0:w, part * NH:(part + 1) * NH],
                                                ktb[c % 2][0:w, part * 512:(part + 1) * 512], start=(part == 0), stop=(part == 2))
                    last.then_inc(s_sc_filled.sem, 1)

                turn(0)
                for c in range(NCH):
                    if c + 1 < NCH:
                        turn(c + 1)
                    score(c)
                s_sc_drained.wait(pe, b, NCH - 1)
                for part in range(3):
                    w = P if part < 2 else ROPE
                    last = nc.tensor.matmul(bank[4 + NCH % 2][0:NH, 0:1], qs[0:w, part * NH:(part + 1) * NH],
                                            qs[0:w, 3 * NH + part:3 * NH + part + 1], start=(part == 0), stop=(part == 2))
                last.then_inc(s_sc_filled.sem, 1)
                s_exp.wait(pe, b)
                s_pt_drained.wait(pe, b, 0)
                pe.sem_inc(gate_pe, 1)
                for pg_ in range(NPAGES):
                    last = nc.tensor.transpose(bank[5][:, pg_ * NH:(pg_ + 1) * NH], WK[0:NH, pg_ * P:(pg_ + 1) * P],
                                               ident[0:NH, 0:NH])
                last.then_inc(s_pt_filled.sem, 1)
                s_prob.wait(pe, b, 2)
                pe.sem_inc(gate_pe, 1)
                nc.tensor.matmul(bank[4][0:NB, 448:448 + NH], psl[0:NH, 0:NB], ident[0:NH, 0:NH], start=True,
                                 stop=True).then_inc(s_pt_filled.sem, 1)
                s_pt_drained.wait(pe, b)
                s_ot_drained.wait(pe, b, 0)
                pe.sem_inc(gate_pe, 1)
                for pg_ in range(NPAGES):
                    last = nc.tensor.matmul(bank[6][0:NH, 0:KVL], ptb[:, pg_ * NH:(pg_ + 1) * NH],
                                            KV[:, pg_ * KVL:(pg_ + 1) * KVL], start=(pg_ == 0), stop=False)
                    if pg_ % 4 == 3:
                        last.then_inc(s_pv.sem, 1)
                nc.tensor.matmul(bank[6][0:NH, 0:KVL], psl[0:NB, NB:2 * NB], z[0:NB, O_CKV:O_KR], start=False,
                                 stop=True).then_inc(s_pv.sem, 1)
                s_ot_drained.wait(pe, b, 1)
                pe.sem_inc(gate_pe, 1)
                for c in range(2):
                    last = nc.tensor.transpose(bank[4][:, c * NH:(c + 1) * NH], o_lat[0:NH, c * P:(c + 1) * P],
                                               ident[0:NH, 0:NH])
                last.then_inc(s_ot_filled.sem, 1)

            attend(0)
            with pe.Fori(1, NB) as b:
                attend(b)
            s_ot_drained.wait(pe, NB - 1)
            for h in range(NH):
                for c in range(2):
                    last = nc.tensor.matmul(bank[6][0:NB, h * VH:(h + 1) * VH], ota[:, (c * NH + h) * NB:(c * NH + h + 1) * NB],
                                            uv[:, c * 512 + h * VH:c * 512 + (h + 1) * VH], start=(c == 0), stop=(c == 1))
            last.then_inc(s_ov_filled, 1)

        ukt = WK[:, 0:2 * NH * P]
        psq = rt

        def pe_experts(pe, t):
            for h in range(PH):
                for _ in range(4):
                    yield "u"
                yield "gelu"
                for q in range(4):
                    for k in range(4 * q + SHARE - 1, 4 * q + 4, SHARE):
                        slot = k % RING
                        diag_ready.wait(pe, t, (h * TOPK + k + 1) // SHARE)
                        pe.wait_ge(row_in[slot], (t * PH + h) * (2 * TOPK // RING) * 16 + (TOPK // RING + k // RING + 1) * 16)
                        for c in range(2):
                            last = nc.tensor.matmul(bank[3 + 4 * c], diag(k), rows[:, slot * D + c * 512:slot * D + (c + 1) * 512],
                                                    start=(h == 0 and k == SHARE - 1), stop=(h == PH - 1 and k == TOPK - 1))
                        last.then_inc(v_pe_used.sem, 1)
                    yield "v"
            yield "fin"

        @block.tensor
        def _(pe):
            pe.wait_ge(const_in, 16 * CONST_LOADS)
            pe.wait_ge(setup_in, 16)
            for i in range(4):
                transposes(KJ, 0, pe, "keys", i, [rows[:, (4 * i + k) * P:(4 * i + k + 1) * P] for k in range(4)])
            pe.wait_ge(KJ.drained, 4)
            pe.sem_inc(keys_read, 1)
            for _ in pe_front(pe, 0):
                pass
            beside(pe_front(pe, 1), pe_experts(pe, 0))
            with pe.Fori(1, T - 1) as t:
                beside(pe_front(pe, t + 1), pe_experts(pe, t))
            beside(pe_front(pe, T, sample=True), iter(()))
            committed.wait(pe, T)
            pe.wait_ge(p_built, 2)
            nc.tensor.transpose(bank[3][:, 0:NB], p_owner, ident[0:NB, 0:NB])
            nc.tensor.transpose(bank[3][:, NB:NB + TOPK], p_rank, ident[0:TOPK, 0:TOPK])
            nc.tensor.matmul(bank[3][:, P:2 * P], p_owner, i0[0:NB, :], start=True, stop=True)
            nc.tensor.matmul(bank[3][:, 2 * P:3 * P], p_owner, pg[0:NB, :], start=True, stop=True)
            for c in range(2):
                last = nc.tensor.matmul(bank[6 + c], p_owner, px[0:NB, c * 512:(c + 1) * 512], start=True, stop=True)
            last.then_inc(p_spread, 1)
            pe.wait_ge(p_coefs, 1)
            pe.wait_ge(p_rows_out, 1)
            pe.wait_ge(p_v_in, 16 * PH)
            for h in range(PH):
                for c in range(2):
                    last = nc.tensor.matmul(bank[6 + c][0:NB, :], p_selc[:, h * NB:(h + 1) * NB], p_v[h][:, c * 512:(c + 1) * 512],
                                            start=(h == 0), stop=(h == PH - 1))
            last.then_inc(p_summed, 1)

        def act_block(act, J, t, tj, name, i, emit):
            w_used.wait(act, t, first[name] + i + 1)
            emit(J.bank(name, i)).then_inc(J.drained, 1)

        def act_drain(act, J, tj, name, i, emit):
            J.wait_filled(act, tj, name, i)
            emit(J.bank(name, i)).then_inc(J.drained, 1)

        copy = nc.scalar.copy

        def act_copy(dst, scale=1.0):
            return lambda b: nc.scalar.activation(dst, b, ACT.Copy, scale=scale)

        def act_front(act, t, sample=False):
            J = AS if sample else A
            tj = 0 if sample else t

            def gained(name, i, dst, gain, count=4):
                J.wait_filled(act, tj, name, i)
                b = J.bank(name, i)
                for k in range(count):
                    g = count * i + k
                    last = nc.scalar.activation(dst[:, g * P:(g + 1) * P], b[:, k * P:(k + 1) * P], ACT.Copy,
                                                scale=gain[:, g:g + 1])
                last.then_inc(J.drained, 1)

            for i in range(2):
                gained("xT", i, xt, attn_gain_t)
            yield "xT"
            for i in range(NA):
                wd = stream[i][3]
                act_block(act, J, t, tj, "linA", i, lambda b: nc.scalar.activation(z[:, i * BW:i * BW + wd], b[:, 0:wd], ACT.Copy))
                yield "lin"
            gained("qlT", 0, t2, q_gain_t, QC)
            act_drain(act, J, tj, "ckT", 0, lambda b: nc.scalar.activation(t2[:, 3 * P:5 * P], b[:, 0:2 * P], ACT.Copy))
            act_drain(act, J, tj, "rqT", 0, lambda b: nc.scalar.activation(rqt, b, ACT.Copy))
            if not sample:
                act_drain(act, J, tj, "rkT", 0, lambda b: nc.scalar.activation(rkt, b, ACT.Copy, scale=float(RDK) ** -0.5))
                act_drain(act, J, tj, "knat", 0, lambda b: nc.scalar.activation(
                    knat[:, :].rearrange("p (h d) -> p h d", h=NH)[:, :, 0:NOPE], b.rearrange("p (h d) -> p h d", h=NH), ACT.Copy))
                if isinstance(t, int) and t == 0:
                    act.wait_ge(zeroed, 2)
                act_drain(act, J, tj, "value", 0, lambda b: nc.scalar.activation(
                    KV[:, ds(t * (NH * VH) + VAT, NH * VH)], b, ACT.Copy))
            yield "lat"
            for i in range(3):
                act_block(act, J, t, tj, "uq", i, lambda b: nc.scalar.activation(qb[:, i * BW:(i + 1) * BW], b[:, 0:BW], ACT.Copy))
                yield "uq"
            if sample:
                act_sample(act)
                yield "reto"
            else:
                for i in range(2):
                    J.wait_filled(act, tj, "reto", i)
                    for h in (2 * i, 2 * i + 1):
                        last = nc.scalar.activation(oret[:, h * RDV:(h + 1) * RDV],
                                                    J.bank("reto", i)[:, (h % 2) * RDV:(h % 2 + 1) * RDV], ACT.Copy,
                                                    accum_out=rstat[:, h:h + 1])
                    last.then_inc(J.drained, 1)
                yield "reto"
            ret_negmean.wait(act, t)
            for h in range(RH):
                last = nc.scalar.activation(junk[:, h * RDV:(h + 1) * RDV],
                                            oret[:, h * RDV:(h + 1) * RDV], ACT.Square,
                                            bias=rstat[:, RH + h:RH + h + 1], accum_out=rstat[:, 2 * RH + h:2 * RH + h + 1])
            last.then_inc(ret_squares.sem, 1)
            yield "squares"
            ret_rstd.wait(act, t)
            for h in range(RH):
                nc.scalar.activation(oret[:, h * RDV:(h + 1) * RDV], oret[:, h * RDV:(h + 1) * RDV], ACT.Identity,
                                     bias=rstat[:, RH + h:RH + h + 1],
                                     scale=rstat[:, 3 * RH + h:3 * RH + h + 1]).then_inc(ret_normed.sem, 1)
            yield "normed"
            if sample:
                act_sample_attention(act)
                yield "keys"
            else:
                for i in range(2):
                    act_drain(act, J, tj, "keyT", i, lambda b: nc.scalar.activation(
                        KV[0:HD, 0:NH * SEQ].rearrange("p (h s) -> p h s", h=NH)[:, 4 * i:4 * i + 4, ds(t * P, P)],
                        b[0:HD, :].rearrange("p (h s) -> p h s", h=4), ACT.Copy))
                for i in range(2):
                    act_drain(act, J, tj, "qT", i, lambda b: nc.scalar.activation(qt[0:HD, 4 * i * P:4 * (i + 1) * P], b[0:HD, :], ACT.Copy))
                yield "keys"
                KT = key_tiles(t)
                for h in range(NH):
                    max_ready.wait(act, t, h + 1)
                    w = NPT * KT * P
                    nc.scalar.activation(sc[h % 2][:, 0:w], sc[h % 2][:, 0:w], ACT.Exp, bias=nmx[:, h:h + 1], scale=SCALE,
                                         accum_out=sums[:, h:h + 1]).then_inc(probs_ready.sem, 1)
                    for i in range(NPT):
                        w = KT * P
                        act_drain(act, J, tj, "probT", NPT * h + i,
                                  lambda b: nc.scalar.activation(pt[:, i * w:(i + 1) * w], b[:, 0:w], ACT.Copy))
                    yield "head"
            for i in range(4):
                w_used.wait(act, t, first["rg"] + i + 1)
                if i == 0:
                    heads_normed.wait(act, t)
                b = J.bank("rg", i)
                nc.scalar.activation(WK[:, i * BW:(i + 1) * BW], b[:, 0:BW], ACT.Tanh, scale=0.5)
                nc.scalar.activation(WK[:, D + i * BW:D + (i + 1) * BW], b[:, 0:BW], ACT.Copy).then_inc(J.drained, 1)
                yield "rg"
            for i in range(2):
                gained("bT", i, t2, ret_gain_t)
            for i in range(4):
                act_block(act, J, t, tj, "ob", i, lambda b: nc.scalar.activation(oret[:, i * BW:(i + 1) * BW], b[:, 0:BW], ACT.Copy))
                yield "ob"
            act_drain(act, J, tj, "ovT", 0, lambda b: nc.scalar.activation(t2[:, 0:512], b, ACT.Copy))
            for i in range(2):
                act_block(act, J, t, tj, "oa", i, lambda b: nc.scalar.activation(oa[:, i * 512:(i + 1) * 512], b, ACT.Copy))
                yield "oa"
            for i in range(8):
                act_block(act, J, t, tj, "gate", i, lambda b: nc.scalar.activation(WK[:, i * BW:(i + 1) * BW], b[:, 0:BW], ACT.Tanh, scale=0.5))
                yield "gate"
            for i in range(2):
                act_drain(act, J, tj, "mT", i, lambda b: nc.scalar.activation(t2[:, 4 * i * P:4 * (i + 1) * P], b, ACT.Copy, scale=0.5))
            yield "merge"
            yield "out"
            for i in range(2):
                act_drain(act, J, tj, "x2T", i, lambda b: nc.scalar.activation(xt[:, 4 * i * P:4 * (i + 1) * P], b, ACT.Copy))
            yield "x2"
            NQ = 2 * PH * PD // BW
            for i in range(NQ):
                w_used.wait(act, t, first["wq"] + i + 1)
                b = J.bank("wq", i)
                for k in range(2):
                    nc.scalar.activation(junk[:, (i % 4) * BW + k * P:(i % 4) * BW + (k + 1) * P], b[:, k * P:(k + 1) * P], ACT.Square,
                                         accum_out=ssq[:, 2 * i + k:2 * i + k + 1])
                nc.scalar.activation(z[:, i * BW:(i + 1) * BW], b[:, 0:BW], ACT.Copy).then_inc(J.drained, 1)
                yield "wq"
            for i in range(4):
                act_drain(act, J, tj, "pqT", i, lambda b: nc.scalar.activation(WK[:, 4 * i * P:4 * (i + 1) * P], b, ACT.Copy))
            yield "pqT"
            for _ in range(TOPK_YIELDS):
                yield "top"
            top_shifted.wait(act, t)
            nc.scalar.activation(gw[:, :], gw[:, :], ACT.Exp).then_inc(top_exp.sem, 1)
            yield "end"

        junk = WK[:, 3 * D:4 * D]

        def act_sample(act):
            act_drain(act, AS, 0, "qnT", 0, lambda b: nc.scalar.activation(psq[0:NOPE, 0:NH * NB], b[0:NOPE, 0:NH * NB], ACT.Copy))
            AS.wait_filled(act, 0, "qrT")
            nc.scalar.activation(nkr[0:ROPE, :], AS.bank("qrT")[0:ROPE, NH * NB:(NH + 1) * NB], ACT.Copy)
            nc.scalar.activation(qabs[0:ROPE, 2 * NH * NB:3 * NH * NB], AS.bank("qrT")[0:ROPE, 0:NH * NB],
                                 ACT.Copy).then_inc(AS.drained, 1)
            s_masked.wait(act, NB - 1)
            for i in range(4):
                act_drain(act, AS, 0, "ukT", i, lambda b: nc.scalar.activation(ukt[0:NOPE, 4 * i * P:4 * (i + 1) * P], b[0:NOPE, :], ACT.Copy))
            act_drain(act, AS, 0, "qabs", 0, lambda b: nc.scalar.activation(qabs[:, 0:2 * NH * NB], b[:, 0:2 * NH * NB], ACT.Copy))
            s_oret_added.wait(act, NB - 1)
            for h in range(RH):
                last = nc.scalar.activation(junk[:, h * RDV:(h + 1) * RDV], oret[:, h * RDV:(h + 1) * RDV], ACT.Copy,
                                            accum_out=rstat[:, h:h + 1])
            last.then_inc(s_ret_sum, 1)

        def act_sample_attention(act):
            AS.wait_drained(act, 0, "qabs")
            ktb = [KV[:, VAT + NPAGES * ROPE + i * 1536:VAT + NPAGES * ROPE + (i + 1) * 1536] for i in range(2)]
            s_state_stored.wait(act, NB - 1)

            def attend(b):
                units = act_head(act, T - 1, b, alone=True)
                s_sc_filled.wait(act, b, 0)
                nc.scalar.activation(qs[:, 0:2 * NH].rearrange("p (c h) -> p c h", c=2),
                                     qabs[:, 0:2 * NH * NB].rearrange("p (c h b) -> p c h b", c=2, h=NH)[:, :, :, ds(b, 1)]
                                     .rearrange("p c h b -> p c (h b)"), ACT.Copy).then_inc(s_staged.sem, 1)
                nc.scalar.activation(qs[0:ROPE, 2 * NH:3 * NH],
                                     qabs[0:ROPE, 2 * NH * NB:3 * NH * NB].rearrange("p (h b) -> p h b", h=NH)[:, :, ds(b, 1)]
                                     .rearrange("p h b -> p (h b)"), ACT.Copy).then_inc(s_staged.sem, 1)
                nc.scalar.activation(qs[:, 3 * NH:3 * NH + 2],
                                     t2[:, 3 * P:5 * P].rearrange("p (c b) -> p c b", c=2)[:, :, ds(b, 1)]
                                     .rearrange("p c b -> p (c b)"), ACT.Copy).then_inc(s_staged.sem, 1)
                nc.scalar.activation(qs[0:ROPE, 3 * NH + 2:3 * NH + 3], nkr[0:ROPE, ds(b, 1)], ACT.Copy).then_inc(s_staged.sem, 1)

                def keys(c):
                    for part in range(3):
                        w = P if part < 2 else ROPE
                        s_kt_filled.wait(act, b, 3 * c + part + 1)
                        if c >= 2 or part >= 0:
                            s_sc_filled.wait(act, b, c - 1)
                        nc.scalar.activation(ktb[c % 2][0:w, part * 512:(part + 1) * 512], bank[part][0:w, :],
                                             ACT.Copy).then_inc(s_kt_drained.sem, 1)

                def score(c):
                    s_sc_filled.wait(act, b, c + 1)
                    if c == 0:
                        s_pt_filled.wait(act, b, 0)
                    w = 512 if c < NCH else 1
                    nc.scalar.activation(WK[0:NH, c * 512:c * 512 + w], bank[4 + c % 2][0:NH, 0:w],
                                         ACT.Copy).then_inc(s_sc_drained.sem, 1)

                keys(0)
                for c in range(NCH):
                    if c + 1 < NCH:
                        keys(c + 1)
                    score(c)
                    next(units, None)
                score(NCH)
                for _ in units:
                    pass
                s_max.wait(act, b)
                nc.scalar.activation(WK[0:NH, 0:NPAGES * P + 1], WK[0:NH, 0:NPAGES * P + 1], ACT.Exp, bias=nmx[0:NH, 0:1],
                                     scale=SCALE, accum_out=sums[0:NH, 0:1]).then_inc(s_exp.sem, 1)
                s_pt_filled.wait(act, b, 1)
                s_pv.wait(act, b, 0)
                nc.scalar.activation(ptb[:, :], bank[5][:, 0:NPAGES * NH], ACT.Copy).then_inc(s_pt_drained.sem, 1)
                s_pt_filled.wait(act, b, 2)
                nc.scalar.activation(psl[0:NB, NB:2 * NB], bank[4][0:NB, 448:448 + NH], ACT.Copy).then_inc(s_pt_drained.sem, 1)
                s_pv.wait(act, b)
                s_ot_filled.wait(act, b, 0)
                nc.scalar.activation(o_lat[0:NH, :], bank[6][0:NH, 0:KVL], ACT.Copy,
                                     scale=sums[0:NH, 1:2]).then_inc(s_ot_drained.sem, 1)
                s_ot_filled.wait(act, b)
                nc.scalar.activation(ota[:, :].rearrange("p (c b) -> p c b", b=NB)[:, :, ds(b, 1)].rearrange("p c b -> p (c b)"),
                                     bank[4][:, 0:2 * NH], ACT.Copy).then_inc(s_ot_drained.sem, 1)

            attend(0)
            with act.Fori(1, NB) as b:
                attend(b)


        V = nc.vector

        def rsqrt(dve, link, x, n, tmp):
            y, u = tmp[:, 0:n], tmp[:, n:2 * n]
            link(dve, V.tensor_scalar(y.bitcast(I32), x.bitcast(I32), -0.5, RSQRT_MAGIC, ALU.mult, ALU.add))
            for _ in range(4):
                link(dve, V.tensor_tensor(u, y, y, ALU.mult))
                link(dve, V.tensor_tensor(u, u, x, ALU.mult))
                link(dve, V.tensor_scalar(u, u, -0.5, 1.5, ALU.mult, ALU.add))
                link(dve, V.tensor_tensor(y, y, u, ALU.mult))
            return y

        def spread(ap, n, width):
            return ap.unsqueeze(2).broadcast_to([P, n, width])

        def over(ap, n, width):
            return ap.unsqueeze(1).broadcast_to([P, n, width])

        def rotate(dve, link, src, dst, tmp_a, tmp_b, n, half, cos, nsin, sin):
            a4 = tmp_a.rearrange("p (n c d) -> p n c d", n=n, c=2)
            b4 = tmp_b.rearrange("p (n c d) -> p n c d", n=n, c=2)
            link.mark(V.tensor_tensor(a4[:, :, 0, :], src[:, :, 0:half], over(cos, n, half), ALU.mult))
            link.mark(V.tensor_tensor(a4[:, :, 1, :], src[:, :, half:2 * half], over(cos, n, half), ALU.mult))
            link.mark(V.tensor_tensor(b4[:, :, 0, :], src[:, :, half:2 * half], over(nsin, n, half), ALU.mult))
            link(dve, V.tensor_tensor(b4[:, :, 1, :], src[:, :, 0:half], over(sin, n, half), ALU.mult))
            return V.tensor_tensor(dst, tmp_a.rearrange("p (n d) -> p n d", n=n), tmp_b.rearrange("p (n d) -> p n d", n=n), ALU.add)

        RD2, MD2 = RDK // 2, ROPE // 2
        r_cos, r_nsin, r_sin = (ropeb[:, i * RD2:(i + 1) * RD2] for i in range(3))
        m_cos, m_nsin, m_sin = (ropeb[:, 3 * RD2 + i * MD2:3 * RD2 + (i + 1) * MD2] for i in range(3))

        def top16(dve, link, src, n, width, vals, idx):
            def every(f):
                dve.sem_inc(gate_dve, 1)
                for g in range(n):
                    link.mark(f(g, src[:, g * width:(g + 1) * width], slice(g * TOPK, g * TOPK + 8), slice(g * TOPK + 8, (g + 1) * TOPK)))
                link.join(dve)
            every(lambda g, s, lo, hi: V.max(vals[:, lo], s))
            yield "top"
            every(lambda g, s, lo, hi: V.max_index(idx[:, lo], vals[:, lo], s))
            yield "top"
            every(lambda g, s, lo, hi: V.match_replace(s, vals[:, lo], s, NEG))
            yield "top"
            every(lambda g, s, lo, hi: V.max(vals[:, hi], s))
            yield "top"
            every(lambda g, s, lo, hi: V.max_index(idx[:, hi], vals[:, hi], s))
            yield "top"

        def dve_front(dve, t, sample=False):
            J, DD = (AS, DS) if sample else (A, DJ)
            tj = 0 if sample else t
            link = fd
            link.begin(t)
            if sample:
                dve.wait_ge(x_in.sem, 48 * T + 32)
            else:
                x_in.wait(dve, t)
            link(dve, V.tensor_tensor_reduce(out=sc[0], in0=xin[:, :], in1=xin[:, :], scale=1.0, scalar=0.0, op0=ALU.mult,
                                             op1=ALU.add, accum_out=stat[:, 0:1]))
            link(dve, V.tensor_scalar(stat[:, 0:1], stat[:, 0:1], 1.0 / D, EPS, ALU.mult, ALU.add))
            r = rsqrt(dve, link, stat[:, 0:1], 1, nr)
            V.tensor_scalar(sc[0], xin[:, :], r, None, ALU.mult).then_inc(x_normed.sem, 1)
            yield "xT"
            for i in range(NA):
                yield "lin"
            J.wait_drained(dve, tj, "linA", NA - 1)
            x_normed.wait(dve, t)
            link.mark(V.tensor_tensor_reduce(out=rt[:, 0:QL], in0=z[:, 0:QL], in1=z[:, 0:QL], scale=1.0, scalar=0.0,
                                             op0=ALU.mult, op1=ALU.add, accum_out=stat[:, 1:2]))
            link(dve, V.tensor_tensor_reduce(out=knat[:, 0:KVL], in0=z[:, O_CKV:O_KR], in1=z[:, O_CKV:O_KR], scale=1.0,
                                             scalar=0.0, op0=ALU.mult, op1=ALU.add, accum_out=stat[:, 2:3]))
            link.mark(V.tensor_scalar(stat[:, 1:2], stat[:, 1:2], 1.0 / QL, EPS, ALU.mult, ALU.add))
            link(dve, V.tensor_scalar(stat[:, 2:3], stat[:, 2:3], 1.0 / KVL, EPS, ALU.mult, ALU.add))
            r = rsqrt(dve, link, stat[:, 1:3], 2, nr)
            link.mark(V.tensor_scalar(z[:, 0:QL], z[:, 0:QL], r[:, 0:1], None, ALU.mult))
            V.scalar_tensor_tensor(out=z[:, O_CKV:O_KR], in0=z[:, O_CKV:O_KR], scalar=r[:, 1:2], in1=kv_gain[:, :],
                                   op0=ALU.mult, op1=ALU.mult).then_inc(lat_normed.sem, 1)
            kr = z[:, O_KR:O_RQ].unsqueeze(1)
            ra = rt[:, 0:ROPE]
            rb = rt[:, ROPE:2 * ROPE]
            link.mark(V.tensor_tensor(ra[:, 0:MD2], z[:, O_KR:O_KR + MD2], m_cos, ALU.mult))
            link.mark(V.tensor_tensor(ra[:, MD2:ROPE], z[:, O_KR + MD2:O_RQ], m_cos, ALU.mult))
            link.mark(V.tensor_tensor(rb[:, 0:MD2], z[:, O_KR + MD2:O_RQ], m_nsin, ALU.mult))
            link(dve, V.tensor_tensor(rb[:, MD2:ROPE], z[:, O_KR:O_KR + MD2], m_sin, ALU.mult))
            V.tensor_tensor(knat[:, :].rearrange("p (h d) -> p h d", h=NH)[:, :, NOPE:HD], over(ra, NH, ROPE),
                            over(rb, NH, ROPE), ALU.add).then_inc(krope_ready.sem, 1)
            rotate(dve, link, z[:, O_RQ:O_RV].rearrange("p (n d) -> p n d", n=2 * RH),
                   rqk.rearrange("p (n d) -> p n d", n=2 * RH), rqk, WK[:, 0:D], 2 * RH, RD2, r_cos, r_nsin, r_sin
                   ).then_inc(ret_roped.sem, 1)
            ret_roped.wait(dve, t)
            if not sample:
                V.tensor_tensor(kd.rearrange("p (h d) -> p h d", h=RH), rqk[:, RH * P:].rearrange("p (h d) -> p h d", h=RH),
                                spread(k_decay[:, :], RH, P), ALU.mult).then_inc(k_decayed.sem, 1)
            yield "lat"
            for i in range(3):
                yield "uq"
            J.wait_drained(dve, tj, "uq", 2)
            krope_ready.wait(dve, t)
            q3 = qb[:, :].rearrange("p (h d) -> p h d", h=NH)[:, :, NOPE:HD]
            rotate(dve, link, q3, q3, rt[:, 0:NH * ROPE], rt[:, NH * ROPE:2 * NH * ROPE], NH, MD2, m_cos, m_nsin, m_sin
                   ).then_inc(q_roped.sem, 1)
            if sample:
                dve_sample_ret(dve)
                dve.wait_ge(s_ret_sum, 1)
            else:
                J.wait_drained(dve, tj, "rqT")
                V.tensor_tensor(rqd, rqt, q_decay[:, :], ALU.mult).then_inc(q_decayed.sem, 1)
                DD.wait_filled(dve, tj, "retA")
                k_decayed.wait(dve, t)
                V.tensor_tensor(at, DD.bank("retA")[:, 0:512], decay_t[:, :], ALU.mult).then_inc(DD.drained, 1)
                DD.wait_filled(dve, tj, "stateU")
                if isinstance(t, int) and t == 0:
                    dve.wait_ge(zeroed, 2)
                for h in range(RH):
                    hs = slice(h * RDV, (h + 1) * RDV)
                    ins = V.scalar_tensor_tensor(out=state[:, hs], in0=state[:, hs], scalar=const["chunk_decay"][h],
                                                 in1=DD.bank("stateU")[:, hs], op0=ALU.mult, op1=ALU.add)
                    if h < RH - 1:
                        link.mark(ins)
                ins.then_inc(DD.drained, 1)
                J.wait_drained(dve, tj, "reto", 1)
            V.tensor_scalar(rstat[:, RH:2 * RH], rstat[:, 0:RH], -1.0 / RDV, None, ALU.mult).then_inc(ret_negmean.sem, 1)
            yield "reto"
            ret_squares.wait(dve, t)
            link(dve, V.tensor_scalar(rstat[:, 2 * RH:3 * RH], rstat[:, 2 * RH:3 * RH], 1.0 / RDV, EPS, ALU.mult, ALU.add))
            r = rsqrt(dve, link, rstat[:, 2 * RH:3 * RH], RH, nr)
            link(dve, V.tensor_copy(rstat[:, 3 * RH:4 * RH], r))
            V.tensor_tensor(rstat[:, RH:2 * RH], rstat[:, RH:2 * RH], r, ALU.mult).then_inc(ret_rstd.sem, 1)
            yield "squares"
            yield "normed"
            if sample:
                dve_sample(dve)
            yield "keys"
            if not sample:
                for h in range(NH):
                    DD.wait_filled(dve, tj, "score", h)
                    if h == 0:
                        ret_normed.wait(dve, t)
                    if h >= 2:
                        A_job_read(dve, t, h - 2)
                    dve.sem_inc(gate_dve, 1)
                    w = NPT * key_tiles(t) * P
                    V.tensor_tensor_reduce(out=sc[h % 2][:, 0:w], in0=DD.bank("score", h)[:, 0:w], in1=maskb[:, 0:w],
                                           scale=1.0, scalar=NEG * 2, op0=ALU.add, op1=ALU.max,
                                           accum_out=mx[:, h:h + 1]).then_inc(DD.drained, 1)
                    DD.wait_drained(dve, tj, "score", h)
                    V.tensor_scalar(nmx[:, h:h + 1], mx[:, h:h + 1], -SCALE, None, ALU.mult).then_inc(max_ready.sem, 1)
                    yield "head"
                probs_ready.wait(dve, t)
                link(dve, V.reciprocal(sums[:, :], sums[:, :]))
                pv_done.wait(dve, t)
                V.tensor_tensor(qb[:, 0:NH * VH].rearrange("p (h d) -> p h d", h=NH),
                                bank[6].rearrange("p (h d) -> p h d", h=NH), spread(sums[:, :], NH, VH),
                                ALU.mult).then_inc(heads_normed.sem, 1)
            for i in range(4):
                yield "rg"
            J.wait_drained(dve, tj, "rg", 3)
            ret_normed.wait(dve, t)
            link(dve, V.scalar_tensor_tensor(out=WK[:, D:2 * D], in0=WK[:, 0:D], scalar=1.0, in1=WK[:, D:2 * D], op0=ALU.add,
                                             op1=ALU.mult))
            V.scalar_tensor_tensor(out=oret[:, :], in0=WK[:, D:2 * D], scalar=0.5, in1=oret[:, :], op0=ALU.mult,
                                   op1=ALU.mult).then_inc(ret_gated.sem, 1)
            for name in ["ob"] * 4 + ["oa"] * 2 + ["gate"] * 8:
                yield name
            J.wait_drained(dve, tj, "gate", 7)
            link.mark(V.scalar_tensor_tensor(out=oa, in0=WK[:, 0:D], scalar=1.0, in1=oa, op0=ALU.add, op1=ALU.mult))
            link(dve, V.scalar_tensor_tensor(out=oret[:, :], in0=WK[:, D:2 * D], scalar=1.0, in1=oret[:, :], op0=ALU.add, op1=ALU.mult))
            V.tensor_tensor(oa, oa, oret[:, :], ALU.add).then_inc(merged.sem, 1)
            yield "merge"
            for i in range(2):
                w_used.wait(dve, t, first["out"] + 2 * i + 2)
                V.tensor_tensor(xin[:, i * 512:(i + 1) * 512], DD.bank("out")[:, 0:512], xin[:, i * 512:(i + 1) * 512],
                                ALU.add).then_inc(DD.drained, 1)
            yield "out"
            DD.wait_drained(dve, tj, "out", 1)
            link(dve, V.tensor_tensor_reduce(out=WK[:, 0:D], in0=xin[:, :], in1=xin[:, :], scale=1.0, scalar=0.0, op0=ALU.mult,
                                             op1=ALU.add, accum_out=stat[:, 3:4]))
            link(dve, V.tensor_scalar(stat[:, 3:4], stat[:, 3:4], 1.0 / D, EPS, ALU.mult, ALU.add))
            r = rsqrt(dve, link, stat[:, 3:4], 1, nr)
            V.scalar_tensor_tensor(out=xn2, in0=xin[:, :], scalar=r, in1=ffn_gain[:, :], op0=ALU.mult,
                                   op1=ALU.mult).then_inc(x2_normed.sem, 1)
            yield "x2"
            for i in range(2 * PH * PD // BW):
                yield "wq"
            J.wait_drained(dve, tj, "wq", 2 * PH * PD // BW - 1)
            x2_normed.wait(dve, t)
            link(dve, V.tensor_scalar(ssq[:, :], ssq[:, :], 1.0 / PD, EPS, ALU.mult, ALU.add))
            r = rsqrt(dve, link, ssq[:, :], 2 * PH, nr)
            yield "pqT"
            for i in range(2):
                DD.wait_filled(dve, tj, "pscore", i)
                V.tensor_tensor(z[:, i * D:(i + 1) * D].rearrange("p (g k) -> p g k", g=PH),
                                DD.bank("pscore", i).rearrange("p (g k) -> p g k", g=PH),
                                spread(r[:, i:2 * PH:2], PH, P), ALU.mult).then_inc(DD.drained, 1)
            DD.wait_drained(dve, tj, "pscore", 1)
            yield from top16(dve, link, z, 2 * PH, P, sv, si)
            link.mark(V.tensor_copy(sif[:, :], si[:, :]))
            cand = z[:, 0:PH * 256]
            for h in range(PH):
                c3 = cand[:, h * 256:(h + 1) * 256].rearrange("p (a b) -> p a b", a=TOPK)
                link.mark(V.tensor_tensor(c3, spread(sv[:, h * TOPK:(h + 1) * TOPK], TOPK, TOPK),
                                          over(sv[:, (PH + h) * TOPK:(PH + h + 1) * TOPK], TOPK, TOPK), ALU.add))
            link.join(dve)
            yield "top"
            yield from top16(dve, link, cand, PH, 256, ts_, tp)
            V.tensor_tensor(gw[:, :].rearrange("p (h k) -> p h k", h=PH), ts_[:, :].rearrange("p (h k) -> p h k", h=PH),
                            ts_[:, :].rearrange("p (h k) -> p h k", h=PH)[:, :, 0:1].broadcast_to([P, PH, TOPK]),
                            ALU.subtract).then_inc(top_shifted.sem, 1)
            for which, (op, arg, dst) in enumerate(((ALU.logical_shift_right, 4, i0), (ALU.bitwise_and, 15, i1))):
                link(dve, V.tensor_scalar(tq[:, :], tp[:, :], arg, None, op))
                link(dve, V.tensor_copy(tf[:, :], tq[:, :]))
                oh = WK[:, 0:P * TOPK]
                link(dve, V.tensor_tensor(oh.rearrange("p (s a) -> p s a", s=P), spread(tf[:, :], P, TOPK),
                                          over(iota16[:, :], P, TOPK), ALU.is_equal))
                for h in range(PH):
                    o3 = oh[:, h * 256:(h + 1) * 256].rearrange("p (k a) -> p k a", k=TOPK)
                    link.mark(V.tensor_tensor(o3, o3, over(sif[:, (which * PH + h) * TOPK:(which * PH + h + 1) * TOPK], TOPK, TOPK), ALU.mult))
                link.join(dve)
                link(dve, V.tensor_reduce(dst[:, :], oh.rearrange("p (s a) -> p s a", s=P), AX, ALU.add))
                yield "top"
            link(dve, V.scalar_tensor_tensor(out=i0[:, :], in0=i0[:, :], scalar=float(NK), in1=i1[:, :], op0=ALU.mult, op1=ALU.add))
            link.mark(V.tensor_copy(eid[:, :], i0[:, :]))
            top_exp.wait(dve, t)
            link(dve, V.tensor_reduce(gs[:, 0:PH], gw[:, :].rearrange("p (h k) -> p h k", h=PH), AX, ALU.add))
            link(dve, V.reciprocal(gs[:, PH:2 * PH], gs[:, 0:PH]))
            V.tensor_tensor(gw[:, :].rearrange("p (h k) -> p h k", h=PH), gw[:, :].rearrange("p (h k) -> p h k", h=PH),
                            spread(gs[:, PH:2 * PH], PH, TOPK), ALU.mult).then_inc(chosen.sem, 1)
            if not sample:
                link.end()
            yield "end"

        def A_job_read(dve, t, h):
            A.wait_filled(dve, t, "probT", NPT * (h + 1) - 1)

        def dve_sample_ret(dve):
            AS.wait_drained(dve, 0, "rqT")
            dve.wait_ge(s_zero, 2)

            def one(b):
                s_outer.wait(dve, b, 0)
                s_oret.wait(dve, b, 0)
                V.tensor_scalar(kmb[0:NB, :], rqk[0:NB, RH * P:2 * RH * P], ret_eye[0:NB, ds(b, 1)], None,
                                ALU.mult).then_inc(s_masked.sem, 1)
                V.tensor_tensor(qmb[:, :].rearrange("p (h b) -> p h b", h=RH),
                                rqt.rearrange("p (h c) -> p h c", h=RH)[:, :, 0:NB],
                                diag8[:, ds(b * NB, NB)].unsqueeze(1).broadcast_to([P, RH, NB]), ALU.mult).then_inc(s_masked.sem, 1)
                s_state_in.wait(dve, b)
                s_outer.wait(dve, b)
                for h in range(RH):
                    hs = slice(h * RDV, (h + 1) * RDV)
                    last = V.scalar_tensor_tensor(out=s_state_buf(b)[:, hs], in0=s_state_buf(b)[:, hs], scalar=const["gamma"][h],
                                                  in1=PS[:, 4 * 512 + h * RDV:4 * 512 + (h + 1) * RDV], op0=ALU.mult, op1=ALU.add)
                last.then_inc(s_state_new.sem, 1)
                s_oret.wait(dve, b)
                s_oret_added.wait(dve, b, 0)
                V.tensor_tensor(oret[0:NB, 0:512], oret[0:NB, 0:512], bank[6][0:NB, :], ALU.add).then_inc(s_oret_added.sem, 1)
                V.tensor_tensor(oret[0:NB, 512:D], oret[0:NB, 512:D], bank[2][0:NB, :], ALU.add).then_inc(s_oret_added.sem, 1)

            q_kmb_free(dve)
            one(0)
            with dve.Fori(1, NB) as b:
                one(b)

        def q_kmb_free(dve):
            AS.wait_drained(dve, 0, "qrT")

        def dve_sample(dve):
            def one(b):
                units = dve_head(dve, T - 1, b, alone=True)
                for c in range(NCH + 1):
                    s_sc_drained.wait(dve, b, c + 1)
                    w = 512 if c < NCH else 1
                    V.tensor_reduce(nr[0:NH, c:c + 1], WK[0:NH, c * 512:c * 512 + w], AX, ALU.max).then_inc(s_max.sem, 1)
                    if c < NCH:
                        next(units, None)
                for _ in units:
                    pass
                s_max.wait(dve, b, NCH + 1)
                V.tensor_reduce(mx[0:NH, 0:1], nr[0:NH, 0:NCH + 1], AX, ALU.max).then_inc(s_max.sem, 1)
                s_max.wait(dve, b, NCH + 2)
                V.tensor_scalar(nmx[0:NH, 0:1], mx[0:NH, 0:1], -SCALE, None, ALU.mult).then_inc(s_max.sem, 1)
                s_exp.wait(dve, b)
                s_ot_drained.wait(dve, b, 0)
                V.tensor_scalar(psl[0:NH, 0:NB], diag8[0:NH, ds(b * NB, NB)], WK[0:NH, NPAGES * P:NPAGES * P + 1], None,
                                ALU.mult).then_inc(s_prob.sem, 1)
                V.reciprocal(sums[0:NH, 1:2], sums[0:NH, 0:1]).then_inc(s_prob.sem, 1)

            assert NB == PH
            committed.wait(dve, T - 1)
            one(0)
            with dve.Fori(1, NB) as b:
                one(b)
            dve.wait_ge(s_ov_filled, 1)
            AS.wait_drained(dve, 0, "qrT")
            V.memset(qb[:, :], 0.0).then_inc(s_zero, 1)
            dve.wait_ge(s_zero, 3)
            V.tensor_copy(qb[0:NB, 0:NH * VH], bank[6][0:NB, :]).then_inc(heads_normed.sem, 1)
            v_dve_used.wait(dve, T - 1)
            v_pe_used.wait(dve, T - 1)
            dve.wait_ge(y_stored, 16 * (T - 1))
            dve.sem_inc(pdl.sem, 2)
            pdl.t, pdl.k = T - 1, 3 + 3 * PH + 2
            dve_final_norm(dve, pdl, P)


        def dve_head(dve, t, h, alone=False):
            link = pdl
            link.t, link.k = t, h * 3 + 3
            for q in range(4):
                for k in range(4 * q, 4 * q + 4):
                    slot = k % RING
                    dve.wait_ge(row_in[slot], h * (2 * TOPK // RING * 16) + t * (PH * 2 * TOPK // RING * 16) + (k // RING + 1) * 16)
                    row = rows[:, slot * D:(slot + 1) * D]
                    V.tensor_tensor_reduce(out=row, in0=row, in1=px[:, :], scale=1.0, scalar=0.0, op0=ALU.mult,
                                           op1=ALU.add, accum_out=dots[:, k:k + 1]).then_inc(u_used.sem, 1)
                yield "u"
            u_used.wait(dve, t, h * TOPK + TOPK)
            link(dve, V.tensor_tensor(ga_[:, :], dots[:, :], dots[:, :], ALU.mult))
            link(dve, V.tensor_scalar(ga_[:, :], ga_[:, :], GELU_A, 1.0, ALU.mult, ALU.add))
            V.tensor_tensor(ga_[:, :], ga_[:, :], dots[:, :], ALU.mult).then_inc(gelu_in.sem, 1)
            gelu_tanh.wait(dve, t, h + 1)
            link(dve, V.scalar_tensor_tensor(out=ga_[:, :], in0=gb_[:, :], scalar=1.0, in1=dots[:, :], op0=ALU.add, op1=ALU.mult))
            (v_pe_used if alone else diag_ready).wait(dve, t, h * (TOPK // SHARE))
            v_dve_used.wait(dve, t, h * (TOPK - TOPK // SHARE))
            V.scalar_tensor_tensor(out=gcoef[:, :], in0=ga_[:, :], scalar=0.5, in1=pg[:, ds(h * TOPK, TOPK)],
                                   op0=ALU.mult, op1=ALU.mult).then_inc(coefs_ready.sem, 1)
            yield "gelu"
            coefs_ready.wait(dve, t, h + 1)
            before = None
            for q in range(4):
                for k in range(4 * q, 4 * q + 4):
                    if k % SHARE == SHARE - 1 and not alone:
                        continue
                    slot = k % RING
                    dve.wait_ge(row_in[slot], h * (2 * TOPK // RING * 16) + t * (PH * 2 * TOPK // RING * 16)
                                + (TOPK // RING + k // RING + 1) * 16)
                    if before is not None:
                        before[0].wait(dve, t, before[1])
                    before = v_row_used(h, k)
                    V.scalar_tensor_tensor(out=py[0][:, :], in0=rows[:, slot * D:(slot + 1) * D], scalar=gcoef[:, k:k + 1],
                                           in1=py[0][:, :], op0=ALU.mult, op1=ALU.add).then_inc(before[0].sem, 1)
                yield "v"

        def dve_experts(dve, t):
            committed.wait(dve, t)
            for h in range(PH):
                yield from dve_head(dve, t, h)
            v_dve_used.wait(dve, t)
            v_pe_used.wait(dve, t)
            pdl.mark(V.tensor_tensor(py[0][:, 0:512], py[0][:, 0:512], bank[3], ALU.add))
            pdl(dve, V.tensor_tensor(py[0][:, 512:D], py[0][:, 512:D], bank[7], ALU.add))
            dve_final_norm(dve, pdl, P)
            pdl.end()
            yield "fin"

        def dve_experts_sample(dve):
            link = pdl
            link.t, link.k = T, 3
            V.tensor_copy(p_owner.rearrange("p (b k) -> p b k", b=NB),
                          ident[0:NB, 0:NB].unsqueeze(2).broadcast_to([NB, NB, TOPK])).then_inc(p_built, 1)
            V.tensor_copy(p_rank.rearrange("p (b k) -> p b k", b=NB),
                          ident[0:TOPK, 0:TOPK].unsqueeze(1).broadcast_to([TOPK, NB, TOPK])).then_inc(p_built, 1)
            dve.wait_ge(p_spread, 1)
            link(dve, V.tensor_copy(p_sel, bank[3][:, 0:NB + TOPK]))
            for at_, dst in ((P, p_idf), (2 * P, p_wt)):
                link(dve, V.tensor_tensor(p_tmp.rearrange("p (h k) -> p h k", h=PH),
                                          bank[3][:, at_:at_ + P].rearrange("p (h k) -> p h k", h=PH),
                                          over(p_sel[:, NB:NB + TOPK], PH, TOPK), ALU.mult))
                link(dve, V.tensor_reduce(dst, p_tmp.rearrange("p (h k) -> p h k", h=PH), AX, ALU.add))
                if dst is p_idf:
                    V.tensor_copy(p_id, p_idf).then_inc(p_ids, 1)
            dve.wait_ge(p_rows_out, 1)
            for h in range(PH):
                dve.wait_ge(p_u_in[h], 16)
                link.mark(V.tensor_tensor_reduce(out=p_u[h], in0=p_u[h], in1=p_x[:, :], scale=1.0, scalar=0.0, op0=ALU.mult,
                                                 op1=ALU.add, accum_out=p_dots[:, h:h + 1]))
            link.join(dve)
            link(dve, V.tensor_tensor(p_ga, p_dots, p_dots, ALU.mult))
            link(dve, V.tensor_scalar(p_ga, p_ga, GELU_A, 1.0, ALU.mult, ALU.add))
            V.tensor_tensor(p_ga, p_ga, p_dots, ALU.mult).then_inc(p_gelu_in, 1)
            dve.wait_ge(p_tanh, 1)
            link(dve, V.scalar_tensor_tensor(out=p_coef, in0=p_gb, scalar=1.0, in1=p_dots, op0=ALU.add, op1=ALU.mult))
            link(dve, V.scalar_tensor_tensor(out=p_coef, in0=p_coef, scalar=0.5, in1=p_wt, op0=ALU.mult, op1=ALU.mult))
            V.tensor_tensor(p_selc.rearrange("p (h b) -> p h b", h=PH), over(p_sel[:, 0:NB], PH, NB),
                            spread(p_coef, PH, NB), ALU.mult).then_inc(p_coefs, 1)
            dve.wait_ge(y_stored, 16 * T)
            dve.wait_ge(p_summed, 1)
            link(dve, V.tensor_tensor(py[0][0:NB, :], py[0][0:NB, :], PS[0:NB, 6 * 512:8 * 512], ALU.add))
            dve_final_norm(dve, link, NB)

        def dve_final_norm(dve, link, n):
            link(dve, V.tensor_tensor_reduce(out=py[1][0:n, :], in0=py[0][0:n, :], in1=py[0][0:n, :], scale=1.0, scalar=0.0,
                                             op0=ALU.mult, op1=ALU.add, accum_out=fin[0:n, 0:1]))
            link(dve, V.tensor_scalar(fin[0:n, 0:1], fin[0:n, 0:1], 1.0 / D, EPS, ALU.mult, ALU.add))
            r = rsqrt(dve, link, fin[0:n, 0:1], 1, fin[0:n, 2:4])
            V.scalar_tensor_tensor(out=py[1][0:n, :], in0=py[0][0:n, :], scalar=r, in1=final_gain[0:n, :], op0=ALU.mult,
                                   op1=ALU.mult).then_inc(y_ready.sem, 1)

        def dve_commit(dve, t):
            pdl.begin(t)
            chosen.wait(dve, t)
            y_ready.wait(dve, t - 1)
            pdl.mark(V.tensor_copy(pe_id[:, :], eid[:, :]))
            pdl.mark(V.tensor_copy(pg[:, :], gw[:, :]))
            pdl.mark(V.tensor_copy(px[:, :], xn2))
            V.tensor_copy(py[0][:, :], xin[:, :]).then_inc(committed.sem, 1)
            committed.wait(dve, t)

        def act_head(act, t, h, alone=False):
            for _ in range(4):
                yield "u"
            gelu_in.wait(act, t, h + 1)
            nc.scalar.activation(gb_[:, :], ga_[:, :], ACT.Tanh, scale=GELU_C).then_inc(gelu_tanh.sem, 1)
            yield "gelu"
            for q in range(4):
                if not alone:
                    coefs_ready.wait(act, t, h + 1)
                    v_pe_used.wait(act, t, h * (TOPK // SHARE))
                    for k in range(4 * q + SHARE - 1, 4 * q + 4, SHARE):
                        nc.scalar.activation(diag(k), ident[:, :], ACT.Copy, scale=gcoef[:, k:k + 1]).then_inc(diag_ready.sem, 1)
                yield "v"

        def act_experts(act, t):
            for h in range(PH):
                for at_ in act_head(act, t, h):
                    yield at_
                    if h == 0 and at_ == "gelu" and not (isinstance(t, int) and t == 0):
                        act.wait_ge(y_stored, t * 16)
            yield "fin"

        @block.scalar
        def _(act):
            act.wait_ge(const_in, 16 * CONST_LOADS)
            for i in range(4):
                KJ.wait_filled(act, 0, "keys", i)
                nc.scalar.activation(keys_t[:, 4 * i * P:4 * (i + 1) * P], KJ.bank("keys", i), ACT.Copy).then_inc(KJ.drained, 1)
            for _ in act_front(act, 0):
                pass
            beside(act_front(act, 1), act_experts(act, 0))
            with act.Fori(1, T - 1) as t:
                beside(act_front(act, t + 1), act_experts(act, t))
            beside(act_front(act, T, sample=True), iter(()))
            act.wait_ge(p_spread, 1)
            nc.scalar.activation(p_x[:, :], PS[:, 6 * 512:8 * 512], ACT.Copy).then_inc(p_rows_out, 1)
            act.wait_ge(p_gelu_in, 1)
            nc.scalar.activation(p_gb, p_ga, ACT.Tanh, scale=GELU_C).then_inc(p_tanh, 1)

        @block.vector
        def _(dve):
            dve.wait_ge(const_in, 16 * CONST_LOADS)
            for _ in dve_front(dve, 0):
                pass
            dve_commit(dve, 0)
            beside(dve_front(dve, 1), dve_experts(dve, 0))
            dve_commit(dve, 1)
            with dve.Fori(1, T - 1) as t:
                beside(dve_front(dve, t + 1), dve_experts(dve, t))
                dve_commit(dve, t + 1)
            V.memset(xin[:, :], 0.0).then_inc(s_zero, 1)
            x2_normed.wait(dve, T - 1)
            V.memset(oret[:, :], 0.0).then_inc(s_zero, 1)
            beside(dve_front(dve, T, sample=True), iter(()))
            dve_commit(dve, T)
            dve_experts_sample(dve)

        third = len(checkpoints) // 3
        assert checkpoints[:third] == checkpoints[third:2 * third] == checkpoints[2 * third:]


FRONT_LINKS = 273
EXPERT_LINKS = 48
CONST_LOADS = 15
TOPK_YIELDS = 13
SHARE = 2


_INS = ['x_prompt', 'x_sample', 'cache_ckv', 'cache_krope', 'state_ret', 'page_table', 'attn_norm_g', 'w_in', 'q_norm_g',
        'w_uq', 'kv_norm_g', 'w_uk', 'w_uv', 'ret_norm_g', 'w_oa', 'w_ob', 'w_out', 'ffn_norm_g', 'peer_w_q',
        'peer_sub_keys', 'peer_u', 'peer_v', 'final_norm_g']


def _constants(seq, past, rope, rdk, rh, nb):
    f = np.float32
    t = seq // P
    pos = np.concatenate([np.arange(seq), np.full(P, past)]).astype(f)

    def angles(d):
        inv = (f(ROPE_BASE) ** (-np.arange(0, d, 2, dtype=f) / f(d))).astype(f)
        ang = (pos[:, None] * inv[None, :]).astype(f).astype(np.float64)
        return [np.cos(ang), -np.sin(ang), np.sin(ang)]

    lg = np.log1p(-np.exp2(-5.0 - np.arange(rh, dtype=f)).astype(f)).astype(np.float64)
    i = np.arange(P)
    rel = i[None, :] - i[:, None]
    decay = np.where(rel[:, None, :] >= 0, np.exp(np.maximum(rel, 0)[:, None, :] * lg[None, :, None]), 0.0)
    q_decay = np.broadcast_to(np.exp((i[None, :] + 1.0) * lg[:, None])[None], (P, rh, P))
    k_decay = np.exp((P - 1.0 - i)[:, None] * lg[None, :]) * float(rdk) ** -0.5
    u = np.arange(2 * seq - P)
    mask = np.where(u[None, :] <= (seq - P) + i[:, None], 0.0, NEG)
    tables = {
        "ident": np.eye(P), "rope": np.concatenate(angles(rdk) + angles(rope), 1), "mask": mask,
        "decay": decay.reshape(P, -1), "q_decay": q_decay.reshape(P, -1), "k_decay": k_decay,
        "iota16": np.broadcast_to(np.arange(TOPK), (P, TOPK)),
        "diag8": np.broadcast_to(np.eye(nb).reshape(1, -1), (P, nb * nb)),
        "ret_eye": np.eye(P, nb) * float(rdk) ** -0.5,
    }
    tables = {k: np.ascontiguousarray(v, dtype=f) for k, v in tables.items()}
    return tables, [float(x) for x in np.exp(P * lg)], [float(x) for x in np.exp(lg)]


def kernel(**inputs):
    import numpy as _np
    import concourse.bacc as _bacc
    from concourse import mybir as _mybir
    from concourse.bass_utils import run_bass_kernel_spmd as _run

    nc = _bacc.Bacc("TRN2", target_bir_lowering=False, num_devices=1)
    arrays, args = {}, {}
    for name in _INS:
        x = _np.ascontiguousarray(inputs[name])
        arrays[f"in_{name}_dram"] = x
        args[name] = nc.dram_tensor(f"in_{name}_dram", x.shape, _mybir.dt.from_np(x.dtype), kind="ExternalInput").ap()
    _, seq, d = inputs["x_prompt"].shape
    nb = inputs["x_sample"].shape[0]
    _, _, page, kvl = inputs["cache_ckv"].shape
    rope = inputs["cache_krope"].shape[3]
    _, _, rh, rdk, rdv = inputs["state_ret"].shape
    tables, chunk_decay, gamma = _constants(seq, inputs["page_table"].shape[1] * page, rope, rdk, rh, nb)
    const = {"chunk_decay": chunk_decay, "gamma": gamma}
    for name, x in tables.items():
        arrays[f"const_{name}_dram"] = x
        const[name] = nc.dram_tensor(f"const_{name}_dram", x.shape, _mybir.dt.from_np(x.dtype), kind="ExternalInput").ap()
    outs = {"y_p": (1, seq, d), "y_s": (nb, 1, d), "ckv_p": (1, 1, seq // page, page, kvl),
            "krope_p": (1, 1, seq // page, page, rope), "ret_p": (1, 1, rh, rdk, rdv), "ckv_s": (1, nb, 1, kvl),
            "krope_s": (1, nb, 1, rope), "ret_s": (1, nb, rh, rdk, rdv)}
    out = {n: nc.dram_tensor(f"out_{n}_dram", s, _mybir.dt.from_np(_np.dtype("float32")), kind="ExternalOutput").ap()
           for n, s in outs.items()}
    program(nc, args, out, const)
    r = _run(nc, [arrays], core_ids=[0])
    return tuple(r.results[0][f"out_{n}_dram"] for n in outs)
```
